# Optimizing a Trainium2 kernel written in Bass

```python
import jax, jax.numpy as jnp
from jax import lax
import numpy as np
import math

D_MODEL = 2048
BATCH = 1
SEQ = 256
DEPTH = 1

CHUNK = 64
D_MIX = D_MODEL
D_A = D_MIX // 2
D_B = D_MIX - D_A
GROUP_DIM = 64
N_GROUPS_A = D_A // GROUP_DIM
N_GROUPS_B = D_B // GROUP_DIM
CONV_A_WIDTH = 3
CONV_B_WIDTH = 31
D_IN = 3 * D_A + 2 * D_B
D_FF = 4 * D_MODEL
EPS = 1e-6


def rms_norm(x, gain):
    xf = x.astype(jnp.float32)
    y = xf * lax.rsqrt(jnp.mean(xf * xf, axis=-1, keepdims=True) + EPS)
    return (y * gain.astype(jnp.float32)).astype(x.dtype)

def layer_norm(x, gain, bias):
    xf = x.astype(jnp.float32)
    mu = jnp.mean(xf, axis=-1, keepdims=True)
    var = jnp.mean(jnp.square(xf - mu), axis=-1, keepdims=True)
    y = (xf - mu) * lax.rsqrt(var + EPS)
    return (y * gain.astype(jnp.float32) + bias.astype(jnp.float32)).astype(x.dtype)

def causal_dwconv(u, w):
    k, c = w.shape
    return lax.conv_general_dilated(
        u, w[:, None, :].astype(u.dtype),
        window_strides=(1,),
        padding=[(k - 1, 0)],
        dimension_numbers=("NWC", "WIO", "NWC"),
        feature_group_count=c,
    )

def first_inputs(seed: int = 0) -> dict:
    key = jax.random.key(seed)
    ks = jax.random.split(key, 16)
    f32 = jnp.float32

    def normal(k, shape, scale):
        return jax.random.normal(k, shape, f32) * scale

    def gain(k, n):
        return jnp.ones((DEPTH, n), f32) + normal(k, (DEPTH, n), 0.02)

    return {
        "x": normal(ks[0], (BATCH, SEQ, D_MODEL), 1.0),
        "mix_pre_gain": gain(ks[1], D_MODEL),
        "w_in": normal(ks[2], (DEPTH, D_MODEL, D_IN), D_MODEL ** -0.5),
        "conv_a_w": normal(ks[3], (DEPTH, CONV_A_WIDTH, D_A), CONV_A_WIDTH ** -0.5),
        "conv_b_w": normal(ks[4], (DEPTH, CONV_B_WIDTH, D_B), CONV_B_WIDTH ** -0.5),
        "conv_b_bias": normal(ks[5], (DEPTH, D_B), 0.02),
        "ln_b_gain": gain(ks[6], D_B),
        "ln_b_bias": normal(ks[7], (DEPTH, D_B), 0.02),
        "w_out": normal(ks[8], (DEPTH, D_MIX, D_MODEL), D_MIX ** -0.5),
        "mix_post_gain": gain(ks[9], D_MODEL),
        "mlp_pre_gain": gain(ks[10], D_MODEL),
        "w_up": normal(ks[11], (DEPTH, D_MODEL, D_FF), D_MODEL ** -0.5),
        "w_down": normal(ks[12], (DEPTH, D_FF, D_MODEL), D_FF ** -0.5),
        "mlp_post_gain": gain(ks[13], D_MODEL),
    }

def first_block(x, mix_pre_gain, w_in, conv_a_w, conv_b_w, conv_b_bias, ln_b_gain,
              ln_b_bias, w_out, mix_post_gain, mlp_pre_gain, w_up, w_down,
              mlp_post_gain):
    h = x
    for l in range(DEPTH):
        u = rms_norm(h, mix_pre_gain[l])
        p = jnp.einsum("bsd,de->bse", u, w_in[l])
        b_gate, c_gate, v_a, val_b, gate_b = jnp.split(
            p, [D_A, 2 * D_A, 3 * D_A, 3 * D_A + D_B], axis=-1)

        y_a = b_gate * causal_dwconv(c_gate * v_a, conv_a_w[l])

        g = val_b * jax.nn.sigmoid(gate_b)
        g = causal_dwconv(g, conv_b_w[l]) + conv_b_bias[l].astype(g.dtype)
        y_b = jax.nn.silu(layer_norm(g, ln_b_gain[l], ln_b_bias[l]))

        mixed = jnp.concatenate([y_a, y_b], axis=-1)
        o = jnp.einsum("bse,ed->bsd", mixed, w_out[l])
        h = h + rms_norm(o, mix_post_gain[l])

        m = rms_norm(h, mlp_pre_gain[l])
        z = jnp.square(jax.nn.relu(jnp.einsum("bsd,df->bsf", m, w_up[l])))
        z = jnp.einsum("bsf,fd->bsd", z, w_down[l])
        h = h + rms_norm(z, mlp_post_gain[l])
    return h


DEPTH_2 = 2

N_A_LAYERS = DEPTH_2 // 2
N_B_LAYERS = DEPTH_2 - N_A_LAYERS
RMS_EPS = 1e-6

E_A = D_MODEL
POOL_WINDOWS = (2, 4, 8, 16)
N_POOL_GROUPS = len(POOL_WINDOWS)
POOL_GROUP_DIM = E_A // N_POOL_GROUPS

HEAD_DIM = 128
HEADS_PER_GROUP = D_MODEL // HEAD_DIM
DILATED_PAIRS = ((128, 1), (512, 4), (2048, 16))
N_DIL_GROUPS = len(DILATED_PAIRS)
E_B = HEADS_PER_GROUP * HEAD_DIM
ROPE_THETA = 10000.0
NEG_INF = -1e30


def rmsnorm(x, g):
    xf = x.astype(jnp.float32)
    inv = lax.rsqrt(jnp.mean(xf * xf, axis=-1, keepdims=True) + RMS_EPS)
    return (xf * inv).astype(x.dtype) * g

def rope_tables(seq):
    inv_freq = 1.0 / (ROPE_THETA ** (jnp.arange(0, HEAD_DIM, 2, dtype=jnp.float32) / HEAD_DIM))
    ang = jnp.arange(seq, dtype=jnp.float32)[:, None] * inv_freq[None, :]
    return jnp.cos(ang), jnp.sin(ang)

def apply_rope(t, cos, sin):
    tf = t.astype(jnp.float32)
    t1, t2 = tf[..., : HEAD_DIM // 2], tf[..., HEAD_DIM // 2:]
    c, s = cos[None, :, None, :], sin[None, :, None, :]
    return jnp.concatenate([t1 * c - t2 * s, t2 * c + t1 * s], axis=-1).astype(t.dtype)

def multiscale_causal_pool(u):
    b, s, _ = u.shape
    u4 = u.reshape(b, s, N_POOL_GROUPS, POOL_GROUP_DIM)
    csum = jnp.cumsum(u4.astype(jnp.float32), axis=1)
    csum = jnp.concatenate([jnp.zeros_like(csum[:, :1]), csum], axis=1)
    win = jnp.asarray(POOL_WINDOWS, dtype=jnp.int32)
    t1 = jnp.arange(1, s + 1, dtype=jnp.int32)[:, None]
    lower = jnp.maximum(t1 - win[None, :], 0)
    c_lo = csum[:, lower, jnp.arange(N_POOL_GROUPS)[None, :], :]
    count = jnp.minimum(t1, win[None, :]).astype(jnp.float32)
    mean = (csum[:, 1:] - c_lo) / count[None, :, :, None]
    return (mean - u4.astype(jnp.float32)).astype(u.dtype)

def dilated_window_attention(q, k, v, window, dilation):
    b, s, h, hd = q.shape
    d = dilation
    nb = window // dilation
    m = s // d
    nblk = -(-m // nb)
    m_pad = nblk * nb

    def residues(t):
        return t.reshape(b, m, d, h, hd).transpose(0, 2, 3, 1, 4)

    qr, kr, vr = residues(q), residues(k), residues(v)
    qb = jnp.pad(qr, ((0, 0), (0, 0), (0, 0), (0, m_pad - m), (0, 0))).reshape(b, d, h, nblk, nb, hd)
    kv_pad = ((0, 0), (0, 0), (0, 0), (nb, m_pad - m), (0, 0))
    kp = jnp.pad(kr, kv_pad).reshape(b, d, h, nblk + 1, nb, hd)
    vp = jnp.pad(vr, kv_pad).reshape(b, d, h, nblk + 1, nb, hd)
    kb = jnp.concatenate([kp[:, :, :, :-1], kp[:, :, :, 1:]], axis=4)
    vb = jnp.concatenate([vp[:, :, :, :-1], vp[:, :, :, 1:]], axis=4)

    scores = jnp.einsum('bdhnqc,bdhnkc->bdhnqk', qb, kb).astype(jnp.float32) * (1.0 / math.sqrt(hd))
    r_idx = jnp.arange(nb)[:, None]
    c_idx = jnp.arange(2 * nb)[None, :]
    band = (c_idx >= r_idx) & (c_idx <= r_idx + nb)
    blk = jnp.arange(nblk)[:, None, None]
    mask = band[None] & (blk * nb + c_idx[None] >= nb)
    scores = jnp.where(mask[None, None, None], scores, NEG_INF)
    lse = jax.nn.logsumexp(scores, axis=-1)
    p = jnp.exp(scores - lse[..., None]).astype(v.dtype)
    out = jnp.einsum('bdhnqk,bdhnkc->bdhnqc', p, vb)

    out = out.reshape(b, d, h, m_pad, hd)[:, :, :, :m]
    lse = lse.reshape(b, d, h, m_pad)[:, :, :, :m]
    out = out.transpose(0, 3, 1, 2, 4).reshape(b, s, h, hd)
    lse = lse.transpose(0, 3, 1, 2).reshape(b, s, h)
    return out, lse

def second_inputs(seed: int = 0) -> dict:
    key = jax.random.key(seed)
    ks = jax.random.split(key, 13)
    f32 = jnp.float32
    x = jax.random.normal(ks[0], (BATCH, SEQ, D_MODEL), f32)
    norm_a = 1.0 + 0.1 * jax.random.normal(ks[1], (N_A_LAYERS, D_MODEL), f32)
    w_in_a = jax.random.normal(ks[2], (N_A_LAYERS, D_MODEL, 2 * E_A), f32) * D_MODEL ** -0.5
    w_grp_a = jax.random.normal(ks[3], (N_A_LAYERS, N_POOL_GROUPS, POOL_GROUP_DIM, POOL_GROUP_DIM), f32) * POOL_GROUP_DIM ** -0.5
    scale_a = 1.0 + 0.1 * jax.random.normal(ks[4], (N_A_LAYERS, E_A), f32)
    w_out_a = jax.random.normal(ks[5], (N_A_LAYERS, E_A, D_MODEL), f32) * E_A ** -0.5
    norm_kv = 1.0 + 0.1 * jax.random.normal(ks[6], (D_MODEL,), f32)
    w_k = jax.random.normal(ks[7], (D_MODEL, E_B), f32) * D_MODEL ** -0.5
    w_v = jax.random.normal(ks[8], (D_MODEL, E_B), f32) * D_MODEL ** -0.5
    norm_b = 1.0 + 0.1 * jax.random.normal(ks[9], (N_B_LAYERS, D_MODEL), f32)
    w_in_b = jax.random.normal(ks[10], (N_B_LAYERS, D_MODEL, N_DIL_GROUPS * E_B + E_B), f32) * D_MODEL ** -0.5
    w_out_b = jax.random.normal(ks[11], (N_B_LAYERS, E_B, D_MODEL), f32) * E_B ** -0.5
    norm_f = 1.0 + 0.1 * jax.random.normal(ks[12], (D_MODEL,), f32)
    return {"x": x, "norm_a": norm_a, "w_in_a": w_in_a, "w_grp_a": w_grp_a, "scale_a": scale_a,
            "w_out_a": w_out_a, "norm_kv": norm_kv, "w_k": w_k, "w_v": w_v, "norm_b": norm_b,
            "w_in_b": w_in_b, "w_out_b": w_out_b, "norm_f": norm_f}

def second_block(x, norm_a, w_in_a, w_grp_a, scale_a, w_out_a, norm_kv, w_k, w_v, norm_b, w_in_b, w_out_b, norm_f):
    b, s, _ = x.shape
    cos, sin = rope_tables(s)
    k_shared = None
    v_shared = None
    for layer in range(DEPTH_2):
        if layer < N_A_LAYERS:
            i = layer
            hdn = rmsnorm(x, norm_a[i])
            proj = hdn @ w_in_a[i]
            u, gate = proj[..., :E_A], proj[..., E_A:]
            pooled = multiscale_causal_pool(u)
            y = jnp.einsum('bsgc,gcd->bsgd', pooled, w_grp_a[i]).reshape(b, s, E_A) * scale_a[i]
            x = x + (y * jax.nn.silu(gate)) @ w_out_a[i]
            if layer == N_A_LAYERS - 1:
                kv_in = rmsnorm(x, norm_kv)
                k_shared = apply_rope((kv_in @ w_k).reshape(b, s, HEADS_PER_GROUP, HEAD_DIM), cos, sin)
                v_shared = (kv_in @ w_v).reshape(b, s, HEADS_PER_GROUP, HEAD_DIM)
        else:
            i = layer - N_A_LAYERS
            hdn = rmsnorm(x, norm_b[i])
            proj = hdn @ w_in_b[i]
            q_all = proj[..., : N_DIL_GROUPS * E_B].reshape(b, s, N_DIL_GROUPS, HEADS_PER_GROUP, HEAD_DIM)
            gate = proj[..., N_DIL_GROUPS * E_B:]
            outs = []
            lses = []
            for g, (window, dilation) in enumerate(DILATED_PAIRS):
                q = apply_rope(q_all[:, :, g], cos, sin)
                o_g, lse_g = dilated_window_attention(q, k_shared, v_shared, window, dilation)
                outs.append(o_g)
                lses.append(lse_g)
            alpha = jax.nn.softmax(jnp.stack(lses, axis=0), axis=0)
            merged = jnp.sum(alpha[..., None].astype(x.dtype) * jnp.stack(outs, axis=0), axis=0)
            merged = merged.reshape(b, s, E_B)
            x = x + (merged * jax.nn.silu(gate)) @ w_out_b[i]
    return rmsnorm(x, norm_f)


def setup_inputs(seed=0):
    out = dict(first_inputs(seed))
    for name, value in second_inputs(seed + 1).items():
        if name != "x":
            out[name + "_2"] = value
    return out


def reference(
    x, mix_pre_gain, w_in, conv_a_w, conv_b_w, conv_b_bias, ln_b_gain, ln_b_bias, w_out,
    mix_post_gain, mlp_pre_gain, w_up, w_down, mlp_post_gain, norm_a_2, w_in_a_2, w_grp_a_2,
    scale_a_2, w_out_a_2, norm_kv_2, w_k_2, w_v_2, norm_b_2, w_in_b_2, w_out_b_2, norm_f_2,
):
    x = first_block(
        x, mix_pre_gain, w_in, conv_a_w, conv_b_w, conv_b_bias, ln_b_gain, ln_b_bias, w_out,
        mix_post_gain, mlp_pre_gain, w_up, w_down, mlp_post_gain,
    )
    return second_block(
        x, norm_a_2, w_in_a_2, w_grp_a_2, scale_a_2, w_out_a_2, norm_kv_2, w_k_2, w_v_2,
        norm_b_2, w_in_b_2, w_out_b_2, norm_f_2,
    )


_drawn_inputs = setup_inputs


def setup_inputs(seed=0):
    import zlib

    import numpy as np

    out = dict(_drawn_inputs(seed))
    spreads = {}
    factors = {'conv_b_bias': 2.733,
     'ln_b_gain': 5.51,
     'ln_b_bias': 6.906,
     'mix_post_gain': 3.548,
     'mlp_pre_gain': 4.074,
     'mlp_post_gain': 4.588,
     'norm_kv_2': 4.753,
     'norm_b_2': 4.571}
    for name, (base, spread) in spreads.items():
        noise = np.random.default_rng([zlib.crc32(name.encode()), seed]).standard_normal(out[name].shape)
        drawn = base * np.exp(spread * noise) if base else spread * noise
        out[name] = __import__('jax').numpy.asarray(drawn.astype(out[name].dtype))
    for name, factor in factors.items():
        out[name] = (out[name] * factor).astype(out[name].dtype)
    return out
```

```python
from contextlib import ExitStack

import numpy as np

import concourse.bass as bass
from concourse import mybir
from concourse.alu_op_type import AluOpType as ALU

F32 = mybir.dt.float32
F32R = mybir.dt.float32r
ACT = mybir.ActivationFunctionType
AX_X = mybir.AxisListType.X

P = 128
TOKENS = 256
HALVES = TOKENS // P
D = 2048
KT = D // P
D_A = D // 2
TILES_A = D_A // P
D_FF = 4 * D
CONV_A = 3
CONV_B = 31
EPS = 1e-6
HEADS = D // P
GROUPS = 3
DILATIONS = (1, 4, 16)
REACH = 128
SCORE_SCALE = 1.0 / float(P) ** 0.5
POOL_WINDOWS = (2, 4, 8, 16)
POOL_PAD = 16
BANK = 512
UNIT = 1024
RAW_SLOTS = 4
SPLIT_SLOTS = 8
NARROW = 256
WIDE = 512
SUPER = 1024
MASKED = -1e30
ROW_CONV_B = 0
ROW_CONV_A = ROW_CONV_B + CONV_B
ROW_BIAS_B = ROW_CONV_A + CONV_A
ROW_LN_GAIN = ROW_BIAS_B + 1
ROW_LN_BIAS = ROW_LN_GAIN + 1
ROW_SCALE = ROW_LN_BIAS + 1
ROWS = ROW_SCALE + 2


class Signal:

    def __init__(self, sem):
        self.sem = sem
        self.count = 0

    def next(self, by):
        self.count += by
        return (self, self.count)


class Queue:

    def __init__(self, done):
        self.done = done
        self.items = []

    def run(self, make, after=(), signal=None, by=1, silent=False):
        waits = [t for t in after if t is not None]
        signal = None if silent else (signal or self.done)
        token = signal.next(by) if signal is not None else None
        self.items.append((waits, make, signal, by))
        return token

    def emit(self, engine):
        reached = {}
        for waits, make, signal, by in self.items:
            for producer, value in waits:
                if reached.get(producer, 0) < value:
                    engine.wait_ge(producer.sem, value)
                    reached[producer] = value
            made = make(engine)
            if signal is not None:
                made.then_inc(signal.sem, by)


class Job:

    def __init__(self, weight, first_tile, tiles, c0, wide):
        self.tiles = tiles
        self.wide = wide
        width = WIDE if wide else NARROW
        self.per_unit = UNIT // width
        self.units = []
        for k in range(first_tile, first_tile + tiles, self.per_unit):
            rows = weight[k * P:(k + self.per_unit) * P, c0:c0 + width]
            self.units.append((rows.rearrange("(k p) n -> p k n", p=P), self.per_unit, width))


def build(nc, t, out):
    ctx = ExitStack()
    with ctx:
        def sb(name, shape, dt=F32):
            return ctx.enter_context(nc.sbuf_tensor(name, shape, dt))

        def signal(name):
            return Signal(ctx.enter_context(nc.semaphore(name)))

        pe = Queue(signal("tensor_done"))
        dve = Queue(signal("vector_done"))
        act = Queue(signal("scalar_done"))
        pool = Queue(signal("gpsimd_done"))
        sp = Queue(None)

        raw = sb("raw_weights", [P, RAW_SLOTS, UNIT])
        high = sb("weights_high", [P, SPLIT_SLOTS, UNIT], F32R)
        low = sb("weights_low", [P, SPLIT_SLOTS, UNIT], F32R)
        act_a = sb("act_a", [P, KT, 2, TOKENS], F32R)
        act_b = sb("act_b", [P, KT, 2, TOKENS], F32R)
        resid = sb("resid", [P, HALVES, D])
        wide_rows = sb("wide_rows", [P, HALVES, D])
        ident = sb("ident", [P, P])
        mean_ones = sb("mean_ones", [P, P])
        feature = sb("feature_columns", [P, TILES_A, ROWS])
        rope = sb("rope", [P, HALVES, 3, P // 2])
        masks = sb("masks", [P, 2, GROUPS * P])
        counts = sb("counts", [P, len(POOL_WINDOWS), POOL_PAD])
        eps = sb("eps", [P, 1])
        sumsq = sb("sumsq", [P, HALVES, 8])
        root = sb("root", [P, HALVES])
        rstd = sb("rstd", [P, HALVES])
        soft = sb("soft", [P, HALVES, 4])
        scratch = sb("scratch", [P, 4096])
        partial = sb("partial", [P, 2, BANK])
        value = sb("value", [P, 2, BANK])

        banks = ctx.enter_context(nc.psum_tensor("job_banks", [P, 4, BANK], F32))
        aux = ctx.enter_context(nc.psum_tensor("aux_banks", [P, 4, BANK], F32))

        raw_ready = [signal(f"raw_ready{i}") for i in range(RAW_SLOTS)]
        const_ready = signal("const_ready")
        x_ready = [signal(f"x_ready{i}") for i in range(HALVES)]
        row_ready = [signal(f"row_ready{i}") for i in range(2)]
        spilled = signal("residual_spilled")
        reloaded = signal("residual_reloaded")
        stored = [signal(f"stored{i}") for i in range(HALVES)]

        w_in, w_out, w_up, w_down = t["w_in"][0], t["w_out"][0], t["w_up"][0], t["w_down"][0]
        w_in_a, w_grp, w_out_a = t["w_in_a_2"][0], t["w_grp_a_2"][0], t["w_out_a_2"][0]
        w_k, w_v, w_in_b, w_out_b = t["w_k_2"], t["w_v_2"], t["w_in_b_2"][0], t["w_out_b_2"][0]

        pairs = D_A // NARROW
        mix_b = [[Job(w_in, 0, KT, base * D_A + i * NARROW, False) for base in (4, 3)] for i in range(pairs)]
        mix_a = [[Job(w_in, 0, KT, base * D_A + i * NARROW, False) for base in (1, 2, 0)] for i in range(pairs)]
        proj = [Job(w_out, 0, KT, c, True) for c in range(0, D, WIDE)]
        supers = D_FF // SUPER
        up = [[Job(w_up, 0, KT, s * SUPER + c, False) for c in range(0, SUPER, NARROW)] for s in range(supers)]
        down = [[Job(w_down, s * SUPER // P, SUPER // P, c, True) for c in range(0, D, WIDE)] for s in range(supers)]
        pool_gate = [Job(w_in_a, 0, KT, D + c, False) for c in range(0, D, NARROW)]
        pool_u = [Job(w_in_a, 0, KT, c, False) for c in range(0, D, NARROW)]
        n_pool = len(POOL_WINDOWS)
        group_dim = D // n_pool
        grp = [[Job(w_grp[g], 0, group_dim // P, c, False) for c in range(0, group_dim, NARROW)]
               for g in range(n_pool)]
        proj_a = [Job(w_out_a, 0, KT, c, True) for c in range(0, D, WIDE)]
        keys = [Job(w_k, 0, KT, c, True) for c in range(0, D, WIDE)]
        vals = [Job(w_v, 0, KT, c, True) for c in range(0, D, WIDE)]
        batches = D // WIDE
        queries = [[Job(w_in_b, 0, KT, g * D + b * WIDE, True) for g in range(GROUPS)] for b in range(batches)]
        gates = [Job(w_in_b, 0, KT, GROUPS * D + c, False) for c in range(0, D, NARROW)]
        proj_b = [Job(w_out_b, 0, KT, c, True) for c in range(0, D, WIDE)]

        order = [j for p_ in mix_b for j in p_] + [j for p_ in mix_a for j in p_] + proj
        order += up[0]
        for s in range(1, supers):
            order += up[s] + down[s - 1]
        order += down[-1] + pool_gate + pool_u + [j for g in grp for j in g] + proj_a
        order += keys + vals + [j for b in queries for j in b] + gates + proj_b
        units = [u for j in order for u in j.units]

        loaded, high_done, low_done, released = [], [], [], []

        def load_unit(n):
            src, k, width = units[n]
            slot = n % RAW_SLOTS
            dst = raw[:, slot, :].rearrange("p (k n) -> p k n", k=k)
            free = [high_done[n - RAW_SLOTS], low_done[n - RAW_SLOTS]] if n >= RAW_SLOTS else []
            loaded.append(sp.run(lambda e: e.dma_start(dst, src), free, raw_ready[slot], 16))

        def split_unit(n):
            r, s = n % RAW_SLOTS, n % SPLIT_SLOTS
            free = released[n - SPLIT_SLOTS] if n >= SPLIT_SLOTS else None
            high_done.append(act.run(lambda e: e.activation(high[:, s, :], raw[:, r, :], ACT.Copy),
                                     [loaded[n], free]))
            low_done.append(dve.run(lambda e: e.tensor_tensor(low[:, s, :], raw[:, r, :], high[:, s, :].bitcast(F32),
                                                              ALU.subtract), [loaded[n], high_done[n], free]))

        def prepare(n):
            while len(low_done) <= min(n, len(units) - 1):
                while len(loaded) <= min(len(low_done) + RAW_SLOTS - 1, len(units) - 1):
                    load_unit(len(loaded))
                split_unit(len(low_done))

        beside = []

        def step():
            if beside:
                try:
                    next(beside[0])
                except StopIteration:
                    beside.pop(0)

        def finish():
            while beside:
                step()

        at = [0]
        turn = [0]
        bank_free = [None] * 4
        ready = {"a": [[] for _ in range(KT)], "b": [[] for _ in range(KT)]}
        act_free = {"a": [None] * KT, "b": [None] * KT}
        bufs = {"a": act_a, "b": act_b}

        def free_unit(token):
            released.append(token)
            prepare(len(released) - 1 + SPLIT_SLOTS)
            step()

        def narrow(job, buf, first=0):
            pair = turn[0] % 2
            turn[0] += 1
            x = bufs[buf]
            last = None
            for u in range(len(job.units)):
                n = at[0]
                at[0] += 1
                s = n % SPLIT_SLOTS
                wh = high[:, s, :].rearrange("p (k n) -> p k n", n=NARROW)
                wl = low[:, s, :].rearrange("p (k n) -> p k n", n=NARROW)
                for k in range(job.per_unit):
                    kt = u * job.per_unit + k
                    for f in range(2):
                        bank = 2 * pair + f
                        cols = slice(f * P, (f + 1) * P)
                        lhs_h, lhs_l = wh[:, k, cols], wl[:, k, cols]
                        waits = [low_done[n]] + ready[buf][first + kt] + ([bank_free[bank]] if kt == 0 else [])
                        o, rhs = banks[:, bank, :], x[:, first + kt, :, :].rearrange("p a n -> p (a n)")
                        pe.run(lambda e, o=o, l=lhs_h, r=rhs, a=(kt == 0): e.matmul(o, l, r, start=a, stop=False),
                               waits, silent=True)
                        o, rhs = banks[:, bank, 0:TOKENS], x[:, first + kt, 0, :]
                        end = k == job.per_unit - 1 and f == 1
                        last = pe.run(lambda e, o=o, l=lhs_l, r=rhs, z=(kt == job.tiles - 1):
                                      e.matmul(o, l, r, start=False, stop=z), silent=not end)
                    act_free[buf][first + kt] = (pe.done, pe.done.count + 1) if k < job.per_unit - 1 else last
                free_unit(last)
            return pair, last

        def wide_products(job, buf, first, pair, n, u, half, signal_end):
            s = n % SPLIT_SLOTS
            wh = high[:, s, :].rearrange("p (k n) -> p k n", n=WIDE)
            wl = low[:, s, :].rearrange("p (k n) -> p k n", n=WIDE)
            bank = 2 * pair + half
            o, x, last = banks[:, bank, :], bufs[buf], None
            for k in range(job.per_unit):
                kt = u * job.per_unit + k
                toks = slice(half * P, (half + 1) * P)
                xh, xl = x[:, first + kt, 0, toks], x[:, first + kt, 1, toks]
                waits = [low_done[n]] + ready[buf][first + kt] + ([bank_free[bank]] if kt == 0 else [])
                for i, (l, r) in enumerate(((xh, wh[:, k, :]), (xh, wl[:, k, :]), (xl, wh[:, k, :]))):
                    end = signal_end and k == job.per_unit - 1 and i == 2
                    last = pe.run(lambda e, l=l, r=r, a=(kt == 0 and i == 0), z=(kt == job.tiles - 1 and i == 2):
                                  e.matmul(o, l, r, start=a, stop=z), waits if i == 0 else (), silent=not end)
            return last

        def wide(job, buf, take, first=0, by_half=False):
            pair = turn[0] % 2
            turn[0] += 1
            n0, count = at[0], len(job.units)
            at[0] += count
            if by_half:
                for u in range(count):
                    last = wide_products(job, buf, first, pair, n0 + u, u, 0, u == count - 1)
                    if u < count - 1:
                        pass
                bank_free[2 * pair] = take(0, banks[:, 2 * pair, :], last)
                for u in range(count):
                    last = wide_products(job, buf, first, pair, n0 + u, u, 1, True)
                    free_unit(last)
                ends = [None, last]
            else:
                for u in range(count):
                    ends = [wide_products(job, buf, first, pair, n0 + u, u, half, half == 1 or u == count - 1)
                            for half in range(HALVES)]
                    free_unit(ends[1])
                bank_free[2 * pair] = take(0, banks[:, 2 * pair, :], ends[0])
            for kt in range(first, first + job.tiles):
                act_free[buf][kt] = ends[1]
            bank_free[2 * pair + 1] = take(1, banks[:, 2 * pair + 1, :], ends[1])

        def split_act(buf, kts, toks, src, after):
            x = bufs[buf]
            hi, lo = x[:, kts, 0, toks], x[:, kts, 1, toks]
            free = [act_free[buf][k] for k in range(kts.start, kts.stop)]
            h = act.run(lambda e: e.activation(hi, src, ACT.Copy), after + free)
            l = dve.run(lambda e: e.tensor_tensor(lo, src, hi.bitcast(F32), ALU.subtract), after + free + [h])
            for k in range(kts.start, kts.stop):
                ready[buf][k] = ready[buf][k] + [h, l] if toks.start else [h, l]
            return l

        def both_banks(pair):
            return banks[:, 2 * pair:2 * pair + 2, :]

        slot_free = [None, None]

        def gather(pair, done):
            ps = both_banks(pair)
            part = partial[:, pair, :].rearrange("p (f n) -> p f n", f=2)
            v = value[:, pair, :].rearrange("p (f n) -> p f n", f=2)
            c = act.run(lambda e: e.activation(part, ps[:, :, TOKENS:2 * TOKENS], ACT.Copy),
                        [done, gathered[pair]])
            s = dve.run(lambda e: e.tensor_tensor(v, ps[:, :, 0:TOKENS], part, ALU.add), [c, slot_free[pair]])
            gathered[pair] = s
            bank_free[2 * pair] = bank_free[2 * pair + 1] = s
            return v, s

        gathered = [None, None]

        def sigmoid(dst, src, after, free=None):
            a = act.run(lambda e: e.activation(dst, src, ACT.Exp, scale=-1.0), after + [free])
            b = dve.run(lambda e: e.tensor_scalar(dst, dst, 1.0, None, ALU.add), [a])
            return dve.run(lambda e: e.reciprocal(dst, dst), [b])

        aux_turn = [0]
        aux_free = [None] * 4

        def inverse_rms(half, parts, after):
            s = sumsq[:, half, 0:parts]
            tot = sumsq[:, half, 7:8]
            a = dve.run(lambda e: e.tensor_reduce(tot, s, AX_X, ALU.add), after)
            b = act.run(lambda e: e.activation(root[:, half:half + 1], tot, ACT.Sqrt, bias=eps[:, 0:1],
                                               scale=1.0 / D), [a])
            return dve.run(lambda e: e.reciprocal(rstd[:, half:half + 1], root[:, half:half + 1]), [b])

        rows = [scratch[:, 0:D], scratch[:, D:2 * D]]
        row_used = [None, None]
        row_loaded = [None, None]

        def load_row(i, src, after):
            row_loaded[i] = sp.run(lambda e: e.dma_start(rows[i], src.partition_broadcast(P)),
                                   after + [row_used[i]], row_ready[i], 16)

        def normalised(half, targets, after, wide_free, pause):
            h, n = resid[:, half, :], wide_rows[:, half, :]
            sq = act.run(lambda e: e.activation(n, h, ACT.Square, accum_out=sumsq[:, half, 0:1]), after + wide_free)
            r = inverse_rms(half, 1, [sq])
            turned = []
            for row, buf in targets:
                s = dve.run(lambda e, row=row: e.scalar_tensor_tensor(n, h, rstd[:, half:half + 1], rows[row],
                                                             ALU.mult, ALU.mult), [r, row_loaded[row]] + turned)
                row_used[row] = s
                for _ in range(pause):
                    yield
                for g in range(KT // 4):
                    b = aux_turn[0] % 4
                    aux_turn[0] += 1
                    for i in range(4):
                        k = 4 * g + i
                        done = pe.run(lambda e, b=b, i=i, k=k: e.transpose(aux[:, b, i * P:(i + 1) * P],
                                                                           n[:, k * P:(k + 1) * P], ident[:, :]),
                                      [s, aux_free[b], consts], silent=i < 3)
                    src = aux[:, b, :].rearrange("p (k n) -> p k n", n=P)
                    aux_free[b] = split_act(buf, slice(4 * g, 4 * g + 4), slice(half * P, half * P + P), src, [done])
                    if pause:
                        yield
                turned = [done]
            turned_done[half] = done

        turned_done = [None, None]
        resid_done = [None, None]

        staging = wide_rows[0:ROWS, 1, 0:D_A]
        small = [(ident[:, :], t["c_ident"]), (rope[:, :, :, :], t["c_rope"]), (masks[:, :, :], t["c_masks"]),
                 (counts[:, :, :], t["c_counts"]),
                 (staging[ROW_CONV_B:ROW_CONV_B + CONV_B, :], t["conv_b_w"][0]),
                 (staging[ROW_CONV_A:ROW_CONV_A + CONV_A, :], t["conv_a_w"][0]),
                 (staging[ROW_BIAS_B:ROW_BIAS_B + 1, :], t["conv_b_bias"]),
                 (staging[ROW_LN_GAIN:ROW_LN_GAIN + 1, :], t["ln_b_gain"]),
                 (staging[ROW_LN_BIAS:ROW_LN_BIAS + 1, :], t["ln_b_bias"]),
                 (staging[ROW_SCALE:ROW_SCALE + 2, :], t["scale_a_2"][0].rearrange("(a n) -> a n", a=2))]
        x_in = t["x"][0].rearrange("(h p) n -> p h n", p=P)
        x_loaded = [act.run(lambda e, i=i: e.dma_start(resid[:, i, :], x_in[:, i, :]), (), x_ready[i], 16)
                    for i in range(HALVES)]
        for dst, src in small:
            consts = act.run(lambda e, dst=dst, src=src: e.dma_start(dst, src), (), const_ready, 16)
        load_row(0, t["mix_pre_gain"][0], [])
        made = dve.run(lambda e: e.memset(eps[:, :], EPS))
        ones_made = dve.run(lambda e: e.memset(mean_ones[:, :], 1.0 / D_A))
        act.run(lambda e: e.activation(root[:, 0:1], eps[:, 0:1], ACT.Copy), [made])

        for j in range(TILES_A):
            tok = pe.run(lambda e, j=j: e.transpose(aux[:, 3, j * ROWS:(j + 1) * ROWS], staging[:, j * P:(j + 1) * P],
                                                    ident[0:ROWS, 0:ROWS]), [consts], silent=j < TILES_A - 1)
        features = dve.run(lambda e: e.tensor_copy(feature[:, :, :].rearrange("p a b -> p (a b)"),
                                                   aux[:, 3, 0:TILES_A * ROWS]), [tok])
        aux_free[3] = features
        prepare(SPLIT_SLOTS - 1)

        for half in range(HALVES):
            for _ in normalised(half, [(0, "a")], [x_loaded[half]], [features], 0):
                pass

        gpad = scratch[:, 0:TILES_A * (TOKENS + CONV_B - 1)].rearrange("p (j n) -> p j n", j=TILES_A)
        o1 = TILES_A * (TOKENS + CONV_B - 1)
        sig = scratch[:, o1:o1 + BANK].rearrange("p (f n) -> p f n", f=2)
        cvpad = scratch[:, o1 + BANK:o1 + BANK + 2 * (TOKENS + CONV_A - 1)].rearrange("p (f n) -> p f n", f=2)
        o2 = o1 + BANK + 2 * (TOKENS + CONV_A - 1)
        conv3 = scratch[:, o2:o2 + BANK].rearrange("p (f n) -> p f n", f=2)
        conv = wide_rows[:, 0, :].rearrange("p (j n) -> p j n", j=TILES_A)
        squares = wide_rows[:, 1, :].rearrange("p (j n) -> p j n", j=TILES_A)
        zero_g = dve.run(lambda e: e.memset(gpad[:, :, 0:CONV_B - 1], 0.0), [row_used[0]])
        zero_c = dve.run(lambda e: e.memset(cvpad[:, :, 0:CONV_A - 1], 0.0), [zero_g])

        def column(row, j):
            return feature[:, j, row:row + 1]

        conv_done = [None] * TILES_A
        mixed_done = []

        def convolve(i, after):
            tiles = (2 * i, 2 * i + 1)
            for j in tiles:
                conv_done[j] = dve.run(lambda e, j=j: e.tensor_scalar(
                    conv[:, j, :], gpad[:, j, 0:TOKENS], column(ROW_CONV_B, j), column(ROW_BIAS_B, j),
                    ALU.mult, ALU.add), after + [turned_done[0]])
            for k in range(1, CONV_B):
                if k % 3 == 0:
                    yield
                for j in tiles:
                    conv_done[j] = dve.run(lambda e, j=j, k=k: e.scalar_tensor_tensor(
                        conv[:, j, :], gpad[:, j, k:k + TOKENS], column(ROW_CONV_B + k, j), conv[:, j, :],
                        ALU.mult, ALU.add), [conv_done[j]])

        def mean_of(src, after, bank):
            for j in range(TILES_A):
                done = pe.run(lambda e, j=j: e.matmul(aux[:, bank, 0:TOKENS], mean_ones[:, :], src[:, j, :],
                                                      start=j == 0, stop=j == TILES_A - 1),
                              after + [aux_free[bank], ones_made], silent=j < TILES_A - 1)
            return done

        def layer_norm():
            m = mean_of(conv, conv_done, 0)
            yield
            for j in range(TILES_A):
                d = dve.run(lambda e, j=j: e.tensor_tensor(conv[:, j, :], conv[:, j, :], aux[:, 0, 0:TOKENS],
                                                           ALU.subtract), [m])
            aux_free[0] = d
            sq = act.run(lambda e: e.activation(squares, conv, ACT.Square), [d, turned_done[1]])
            yield
            v = mean_of(squares, [sq], 1)
            yield
            inv = lnorm
            a = act.run(lambda e: e.activation(inv, aux[:, 1, 0:TOKENS], ACT.Sqrt, bias=eps[:, 0:1]), [v])
            b = dve.run(lambda e: e.reciprocal(inv, inv), [a])
            aux_free[1] = a
            yield
            for i in range(TILES_A // 2):
                toks = []
                for j in (2 * i, 2 * i + 1):
                    c = dve.run(lambda e, j=j: e.tensor_tensor(conv[:, j, :], conv[:, j, :], inv, ALU.mult), [b])
                    toks.append(dve.run(lambda e, j=j: e.tensor_scalar(
                        conv[:, j, :], conv[:, j, :], column(ROW_LN_GAIN, j), column(ROW_LN_BIAS, j),
                        ALU.mult, ALU.add), [c]))
                two = slice(2 * i, 2 * i + 2)
                s = sigmoid(squares[:, two, :], conv[:, two, :], toks, v)
                y = dve.run(lambda e, two=two: e.tensor_tensor(squares[:, two, :], squares[:, two, :],
                                                               conv[:, two, :], ALU.mult), [s])
                mixed_done.append(split_act("b", slice(TILES_A + 2 * i, TILES_A + 2 * i + 2), slice(0, TOKENS),
                                            squares[:, two, :], [y]))
                yield

        lnorm = gpad[:, 0, 0:TOKENS]
        g_done = None
        for i in range(pairs):
            gate_job, val_job = mix_b[i]
            pair, done = narrow(gate_job, "a")
            v, s = gather(pair, done)
            sg = sigmoid(sig, v, [s], g_done or zero_c)
            slot_free[pair] = sg
            pair, done = narrow(val_job, "a")
            v, s = gather(pair, done)
            dst = gpad[:, 2 * i:2 * i + 2, CONV_B - 1:]
            g_done = dve.run(lambda e, v=v, dst=dst: e.tensor_tensor(dst, v, sig, ALU.mult), [s, sg, zero_g])
            slot_free[pair] = g_done
            beside.append(convolve(i, [g_done, zero_g, features]))
        beside.append(layer_norm())

        cv_free = None
        for i in range(pairs):
            c_job, v_job, b_job = mix_a[i]
            pair_c, done = narrow(c_job, "a")
            vc, sc = gather(pair_c, done)
            cp = dve.run(lambda e, vc=vc: e.tensor_copy(cvpad[:, :, CONV_A - 1:], vc), [sc, zero_c, cv_free])
            slot_free[pair_c] = cp
            pair, done = narrow(v_job, "a")
            vv, s = gather(pair, done)
            cv = dve.run(lambda e, vv=vv: e.tensor_tensor(cvpad[:, :, CONV_A - 1:], cvpad[:, :, CONV_A - 1:], vv,
                                                          ALU.mult), [s, cp])
            slot_free[pair] = cv
            toks = []
            for f in range(2):
                j = 2 * i + f
                a = dve.run(lambda e, f=f, j=j: e.tensor_scalar(conv3[:, f, :], cvpad[:, f, 0:TOKENS],
                                                                column(ROW_CONV_A, j), None, ALU.mult),
                            [cv, cv_free])
                for k in range(1, CONV_A):
                    a = dve.run(lambda e, f=f, j=j, k=k: e.scalar_tensor_tensor(
                        conv3[:, f, :], cvpad[:, f, k:k + TOKENS], column(ROW_CONV_A + k, j), conv3[:, f, :],
                        ALU.mult, ALU.add), [a])
                toks.append(a)
            pair, done = narrow(b_job, "a")
            vb, s = gather(pair, done)
            y = dve.run(lambda e, vb=vb: e.tensor_tensor(conv3, vb, conv3, ALU.mult), [s] + toks)
            slot_free[pair] = y
            cv_free = split_act("b", slice(2 * i, 2 * i + 2), slice(0, TOKENS), conv3, [y])
        finish()

        load_row(0, t["mix_post_gain"][0], [cv_free] + mixed_done)
        load_row(1, t["mlp_pre_gain"][0], [cv_free] + mixed_done)

        def keep_rows(c, parts_done, wide_free):
            def take(half, ps, done):
                cols = slice(c * WIDE, (c + 1) * WIDE)
                dst = wide_rows[:, half, cols]
                a = dve.run(lambda e: e.tensor_copy(dst, ps), [done] + wide_free)
                b = act.run(lambda e: e.activation(ps, ps, ACT.Square, accum_out=sumsq[:, half, c:c + 1]),
                            [a])
                parts_done[half] += [a, b]
                return b
            return take

        def add_normed(half, parts, targets, pause):
            n, h = wide_rows[:, half, :], resid[:, half, :]
            r = inverse_rms(half, D // WIDE, parts)
            a = dve.run(lambda e: e.scalar_tensor_tensor(n, n, rstd[:, half:half + 1], rows[0],
                                                         ALU.mult, ALU.mult), [r, row_loaded[0]])
            row_used[0] = a
            resid_done[half] = dve.run(lambda e: e.tensor_tensor(h, h, n, ALU.add), [a])
            yield from normalised(half, targets, [resid_done[half]], [], pause)

        parts = [[], []]
        for c, job in enumerate(proj):
            final = c == len(proj) - 1
            take = keep_rows(c, parts, mixed_done)

            def take_last(half, ps, done, take=take):
                b = take(half, ps, done)
                if half == 0:
                    beside.append(add_normed(0, parts[0], [(1, "a")], 4))
                return b
            wide(job, "b", take_last if final else take, by_half=final)
        beside.append(add_normed(1, parts[1], [(1, "a")], 0))
        finish()
        load_row(0, t["mlp_post_gain"][0], [])
        load_row(1, t["norm_a_2"][0], [])

        z_tiles = SUPER // P

        def up_part(s):
            for c, job in enumerate(up[s]):
                pair, done = narrow(job, "a")
                v, a = gather(pair, done)
                z = dve.run(lambda e, v=v: e.scalar_tensor_tensor(v, v, 0.0, v, ALU.max, ALU.mult), [a])
                k = (s % 2) * z_tiles + 2 * c
                slot_free[pair] = split_act("b", slice(k, k + 2), slice(0, TOKENS), v, [z])

        mlp_parts = [[], []]

        def down_part(s):
            for c, job in enumerate(down[s]):
                cols = slice(c * WIDE, (c + 1) * WIDE)
                last_part = s == supers - 1
                final = last_part and c == len(down[s]) - 1

                def take(half, ps, done, c=c, cols=cols, final=final):
                    dst = wide_rows[:, half, cols]
                    if s == 0:
                        a = dve.run(lambda e: e.tensor_copy(dst, ps), [done, turned_done[half]])
                    else:
                        a = dve.run(lambda e: e.tensor_tensor(dst, dst, ps, ALU.add), [done, row_part[half][c]])
                    row_part[half][c] = a
                    if last_part:
                        b = act.run(lambda e: e.activation(ps, dst, ACT.Square, accum_out=sumsq[:, half, c:c + 1]),
                                    [a])
                        mlp_parts[half].extend([a, b])
                        if final and half == 0:
                            beside.append(add_normed(0, mlp_parts[0], [(1, "a")], 3))
                        return b
                    return a
                wide(job, "b", take, first=(s % 2) * z_tiles, by_half=final)

        row_part = [[None] * (D // WIDE) for _ in range(HALVES)]
        up_part(0)
        for s in range(1, supers):
            up_part(s)
            down_part(s - 1)
        down_part(supers - 1)
        beside.append(add_normed(1, mlp_parts[1], [(1, "a")], 0))
        finish()

        silu_gate = wide_rows[:, :, :].rearrange("p h (j n) -> p (h j) n", n=TOKENS)
        gate_done = [None] * KT
        for i, job in enumerate(pool_gate):
            pair, done = narrow(job, "a")
            v, s = gather(pair, done)
            dst = silu_gate[:, 2 * i:2 * i + 2, :]
            sg = sigmoid(dst, v, [s] + turned_done)
            a = dve.run(lambda e, v=v, dst=dst: e.tensor_tensor(dst, dst, v, ALU.mult), [sg])
            slot_free[pair] = a
            gate_done[2 * i] = gate_done[2 * i + 1] = a

        tiles_g = group_dim // P
        padded = TOKENS + POOL_PAD
        trio = [scratch[:, i * tiles_g * padded:(i + 1) * tiles_g * padded].rearrange("p (j n) -> p j n", j=tiles_g)
                for i in range(3)]
        u_buf, sum_a, sum_b = trio
        zero = [dve.run(lambda e, b=b: e.memset(b[:, :, 0:POOL_PAD], 0.0), row_used) for b in trio]
        pool_free = zero[-1]
        jobs_g = group_dim // NARROW
        for g, window in enumerate(POOL_WINDOWS):
            got = []
            for i in range(jobs_g):
                pair, done = narrow(pool_u[g * jobs_g + i], "a")
                v, s = gather(pair, done)
                dst = u_buf[:, 2 * i:2 * i + 2, POOL_PAD:]
                a = dve.run(lambda e, v=v, dst=dst: e.tensor_copy(dst, v), [s, pool_free])
                slot_free[pair] = a
                got.append(a)

            def window_means(g=g, window=window, got=got):
                src, shift, toks, spare = u_buf, 1, got, [sum_a, sum_b]
                while shift < window:
                    dst = spare[0]
                    a = dve.run(lambda e, d=dst, s=src, k=shift: e.tensor_tensor(
                        d[:, :, POOL_PAD:], s[:, :, POOL_PAD:], s[:, :, POOL_PAD - k:POOL_PAD - k + TOKENS], ALU.add),
                        toks + [pool_free, zero[-1]])
                    spare = [spare[1], dst]
                    src, toks, shift = dst, [a], 2 * shift
                    yield
                other = spare[0]
                early = POOL_PAD
                a = dve.run(lambda e: e.scalar_tensor_tensor(
                    other[:, :, POOL_PAD + early:], src[:, :, POOL_PAD + early:], 1.0 / window,
                    u_buf[:, :, POOL_PAD + early:], ALU.mult, ALU.subtract), toks)
                for j in range(tiles_g):
                    b = dve.run(lambda e, j=j: e.tensor_tensor(other[:, j, POOL_PAD:POOL_PAD + early],
                                                               src[:, j, POOL_PAD:POOL_PAD + early],
                                                               counts[:, g, :], ALU.mult), toks)
                b = dve.run(lambda e: e.tensor_tensor(other[:, :, POOL_PAD:POOL_PAD + early],
                                                      other[:, :, POOL_PAD:POOL_PAD + early],
                                                      u_buf[:, :, POOL_PAD:POOL_PAD + early], ALU.subtract), [b])
                pooled.append(split_act("b", slice(g * tiles_g, (g + 1) * tiles_g), slice(0, TOKENS),
                                        other[:, :, POOL_PAD:], [a, b]))

            pooled = []
            for _ in window_means():
                pass
            pool_free = pooled[0]

        for g in range(n_pool):
            for i, job in enumerate(grp[g]):
                pair, done = narrow(job, "b", first=g * tiles_g)
                v, s = gather(pair, done)
                k = g * tiles_g + 2 * i
                for f in range(2):
                    j = k + f
                    a = dve.run(lambda e, f=f, j=j, v=v: e.scalar_tensor_tensor(
                        v[:, f, :], v[:, f, :], column(ROW_SCALE + j // TILES_A, j % TILES_A), silu_gate[:, j, :],
                        ALU.mult, ALU.mult), [s, gate_done[j]])
                slot_free[pair] = split_act("a", slice(k, k + 2), slice(0, TOKENS), v, [a])

        load_row(0, t["norm_kv_2"], [pool_free])
        load_row(1, t["norm_b_2"][0], [pool_free])
        for c, job in enumerate(proj_a):
            final = c == len(proj_a) - 1

            def take(half, ps, done):
                h = resid[:, half, c * WIDE:(c + 1) * WIDE]
                a = dve.run(lambda e: e.tensor_tensor(h, h, ps, ALU.add), [done])
                if final and half == 0:
                    beside.append(normalised(0, [(0, "a"), (1, "b")], [a], [gate_last], 3))
                last_add[half] = a
                return a
            last_add = [None, None]
            gate_last = a_gate = slot_free[pair]
            wide(job, "a", take, by_half=final)
        beside.append(normalised(1, [(0, "a"), (1, "b")], [last_add[1]], [gate_last], 0))
        finish()
        resid_dram = t["residual"].rearrange("(h p) n -> p h n", p=P)
        spill = sp.run(lambda e: e.dma_start(resid_dram, resid[:, :, :]), [row_used[1]], spilled, 16)

        scores_free = {"turn": None}
        key_t = resid[:, :, :].rearrange("p h (j n) -> p (h j) n", n=TOKENS)
        query_t = scratch[:, 0:GROUPS * 4 * TOKENS].rearrange("p (g j n) -> p g j n", g=GROUPS, j=4)
        heads_per = WIDE // P
        half_d = P // 2
        rope_tok = {"free": None}

        def rotated(half, ps, done, dst, free):
            x = ps.rearrange("p (h a n) -> p h a n", h=heads_per, a=2)
            a_, b_ = (partial[:, i, :].rearrange("p (h a n) -> p h a n", h=heads_per, a=2) for i in range(2))
            cos, neg, pos = (rope[:, half, i, :] for i in range(3))

            def tab(w, n):
                shape = [P, heads_per, half_d]
                return w.unsqueeze(1).to_broadcast(shape)
            o = []
            for a in range(2):
                o.append(dve.run(lambda e, a=a: e.tensor_tensor(a_[:, :, a, :], x[:, :, a, :], tab(cos, 0), ALU.mult),
                                 [done, rope_tok["free"], consts] + gathered))
                o.append(dve.run(lambda e, a=a: e.tensor_tensor(b_[:, :, a, :], x[:, :, 1 - a, :],
                                                                tab(neg if a == 0 else pos, 0), ALU.mult), [done]))
            r = value[:, 0, :]
            s = dve.run(lambda e: e.tensor_tensor(r, partial[:, 0, :], partial[:, 1, :], ALU.add),
                        o + [rope_tok["turned"]])
            rope_tok["free"] = s

            def turn_heads():
                yield
                for i in range(heads_per):
                    d = pe.run(lambda e, i=i: e.transpose(aux[:, 3, i * P:(i + 1) * P], r[:, i * P:(i + 1) * P],
                                                          ident[:, :]), [s, aux_free[3]], silent=i < heads_per - 1)
                rope_tok["turned"] = d
                c = act.run(lambda e: e.activation(dst, aux[:, 3, :].rearrange("p (h n) -> p h n", h=heads_per),
                                                   ACT.Copy), [d] + free)
                aux_free[3] = c
                rope_tok["copied"].append(c)
            return s, turn_heads

        rope_tok["turned"] = slot_free[0]
        rope_tok["copied"] = []
        hold = {}

        def take_rotated(dst_of, free):
            def take(half, ps, done):
                s, turn_heads = rotated(half, ps, done, dst_of(half), free)
                if half == 0:
                    for _ in turn_heads():
                        pass
                else:
                    for _ in turn_heads():
                        pass
                return s
            return take

        for c, job in enumerate(keys):
            wide(job, "a", take_rotated(
                lambda half, c=c: key_t[:, c * heads_per:(c + 1) * heads_per, half * P:(half + 1) * P], [spill]))
        keys_done = rope_tok["copied"][-1]

        v_rows = wide_rows
        for c, job in enumerate(vals):
            def take(half, ps, done):
                dst = v_rows[:, half, c * WIDE:(c + 1) * WIDE]
                hold["v"] = act.run(lambda e: e.activation(dst, ps, ACT.Copy), [done] + turned_done)
                return hold["v"]
            wide(job, "a", take)
        values_done = hold["v"]

        e_buf = scratch[:, 3072:3072 + 768].rearrange("p (b n) -> p b n", b=2)
        p_buf = scratch[:, 3840:3840 + 256].rearrange("p (b n) -> p b n", b=2)
        pt_buf = value[:, 1, 0:3 * P]
        prev = {"e": None, "p": None, "pt": slot_free[1], "s0": None, "s1": None}
        query_free = {"t": None}

        def attend(head, j, q_done):
            base = [[0], [1, 2]]
            p_turned = []
            scored = []
            for half in range(HALVES):
                for blk in range(half + 1):
                    bank = base[half][blk]
                    for g in range(GROUPS):
                        d = pe.run(lambda e, g=g, bank=bank, half=half, blk=blk: e.matmul(
                            aux[:, bank, g * P:(g + 1) * P], query_t[:, g, j, half * P:(half + 1) * P],
                            key_t[:, head, blk * P:(blk + 1) * P], start=True, stop=True),
                            q_done + [keys_done, aux_free[bank]], silent=g < GROUPS - 1)
                scored.append(d)
            query_free["t"] = scored[1]
            yield
            for half in range(HALVES):
                nb = half + 1
                b0 = base[half][0]
                ps = aux[:, b0:b0 + nb, 0:GROUPS * P]
                mask = masks[:, 2 - nb:2, :]
                e_ = e_buf[:, 0:nb, :]
                st = soft[:, half, :]
                a = dve.run(lambda e, ps=ps, mask=mask, e_=e_: e.scalar_tensor_tensor(
                    e_, ps, SCORE_SCALE, mask, ALU.mult, ALU.add), [scored[half], prev["e"]])
                for b in range(b0, b0 + nb):
                    aux_free[b] = a
                m = dve.run(lambda e, e_=e_, st=st: e.tensor_reduce(st[:, 0:1], e_, mybir.AxisListType.XY, ALU.max),
                            [a, prev["e"]])
                m = dve.run(lambda e, st=st: e.tensor_scalar(st[:, 1:2], st[:, 0:1], -1.0, None, ALU.mult), [m])
                x = act.run(lambda e, e_=e_, st=st: e.activation(e_, e_, ACT.Exp, bias=st[:, 1:2],
                                                                 accum_out=st[:, 2:3]), [m])
                yield
                r = dve.run(lambda e, st=st: e.reciprocal(st[:, 3:4], st[:, 2:3]), [x])
                p_ = p_buf[:, 0:nb, :]
                e3 = e_buf[:, 0:nb, :].rearrange("p b (g n) -> p b g n", g=GROUPS)
                q1 = dve.run(lambda e, p_=p_, e3=e3: e.tensor_tensor(p_, e3[:, :, 0, :], e3[:, :, 1, :], ALU.add),
                             [x, prev["p"]])
                q2 = dve.run(lambda e, p_=p_, e3=e3: e.tensor_tensor(p_, p_, e3[:, :, 2, :], ALU.add), [q1])
                prev["e"] = q2
                q3 = dve.run(lambda e, p_=p_, st=st: e.tensor_scalar(p_, p_, st[:, 3:4], None, ALU.mult), [r, q2])
                yield
                for blk in range(nb):
                    col = (half if blk == 0 else 2) * P
                    d = pe.run(lambda e, blk=blk, col=col: e.transpose(aux[:, 3, col:col + P], p_buf[:, blk, :],
                                                                       ident[:, :]),
                               [q3, aux_free[3]], silent=blk < nb - 1)
                prev["p"] = d
                lo, hi = (0, P) if half == 0 else (P, 3 * P)
                c = act.run(lambda e, lo=lo, hi=hi: e.activation(pt_buf[:, lo:hi], aux[:, 3, lo:hi], ACT.Copy),
                            [d, prev["pt"]])
                aux_free[3] = c
                p_turned.append(c)
            yield
            cols = slice(head * P, (head + 1) * P)
            pe.run(lambda e: e.matmul(aux[:, 0, 0:TOKENS], v_rows[:, 0, cols], pt_buf[:, 0:2 * P],
                                      start=True, stop=False), p_turned + [aux_free[0], values_done], silent=True)
            d = pe.run(lambda e: e.matmul(aux[:, 0, P:2 * P], v_rows[:, 1, cols], pt_buf[:, 2 * P:3 * P],
                                          start=False, stop=True))
            prev["pt"] = d
            aux_free[0] = split_act("a", slice(head, head + 1), slice(0, TOKENS),
                                    aux[:, 0:1, 0:TOKENS], [d])
            yield

        for b in range(batches):
            q_tokens = []
            for g, job in enumerate(queries[b]):
                rope_tok["copied"] = []
                wide(job, "b", take_rotated(
                    lambda half, g=g: query_t[:, g, :, half * P:(half + 1) * P], [query_free["t"], row_used[1]]))
                q_tokens += rope_tok["copied"]
                if g == 0:
                    pass
                if g == 0 and b > 0:
                    pass
            for j in range(heads_per):
                beside.append(attend(b * heads_per + j, j, q_tokens))
            if b < batches - 1:
                finish()

        rope_end = rope_tok["turned"]
        slot_free[0] = rope_end
        gate_val = []
        sg_buf = scratch[:, 0:BANK].rearrange("p (f n) -> p f n", f=2)
        finish()
        for i, job in enumerate(gates):
            pair, done = narrow(job, "b")
            v, s = gather(pair, done)
            sg = sigmoid(sg_buf, v, [s], hold.get("sg") or query_free["t"])
            a = dve.run(lambda e, v=v: e.tensor_tensor(v, v, sg_buf, ALU.mult), [sg])
            k = slice(2 * i, 2 * i + 2)
            whole = dve.run(lambda e, k=k: e.tensor_tensor(sg_buf, act_a[:, k, 0, :].bitcast(F32),
                                                           act_a[:, k, 1, :].bitcast(F32), ALU.add),
                            [a] + ready["a"][2 * i] + ready["a"][2 * i + 1])
            y = dve.run(lambda e, v=v: e.tensor_tensor(v, v, sg_buf, ALU.mult), [whole])
            hold["sg"] = y
            slot_free[pair] = split_act("a", k, slice(0, TOKENS), v, [y])

        load_row(0, t["norm_f_2"], [hold["sg"], prev["e"]])
        reload_ = sp.run(lambda e: e.dma_start(resid[:, :, :], resid_dram), [spill, query_free["t"]], reloaded, 16)
        out_v = out.rearrange("b (h p) n -> p (b h) n", p=P)
        adds = [[], []]

        def final_norm(half):
            h, n = resid[:, half, :], wide_rows[:, half, :]
            sq = act.run(lambda e: e.activation(n, h, ACT.Square, accum_out=sumsq[:, half, 0:1]),
                         adds[half] + [prev["pt"]])
            r = inverse_rms(half, 1, [sq])
            s = dve.run(lambda e: e.scalar_tensor_tensor(n, h, rstd[:, half:half + 1], rows[0],
                                                         ALU.mult, ALU.mult), [r, row_loaded[0]])
            sp.run(lambda e: e.dma_start(out_v[:, half, :], n), [s], stored[half], 16)

        for c, job in enumerate(proj_b):
            final = c == len(proj_b) - 1

            def take(half, ps, done):
                h = resid[:, half, c * WIDE:(c + 1) * WIDE]
                a = dve.run(lambda e: e.tensor_tensor(h, h, ps, ALU.add), [done, reload_])
                adds[half].append(a)
                if final and half == 0:
                    final_norm(0)
                return a
            wide(job, "a", take, by_half=final)
        final_norm(1)
        sp.run(lambda e: e.wait_ge(spilled.sem, spilled.count), [(stored[0], 16), (stored[1], 16)], silent=True)

        block = ctx.enter_context(nc.Block())

        @block.sync
        def _(e):
            sp.emit(e)

        @block.scalar
        def _(e):
            act.emit(e)

        @block.vector
        def _(e):
            dve.emit(e)

        @block.tensor
        def _(e):
            pe.emit(e)


_INS = ["x", "mix_pre_gain", "w_in", "conv_a_w", "conv_b_w", "conv_b_bias", "ln_b_gain", "ln_b_bias", "w_out",
        "mix_post_gain", "mlp_pre_gain", "w_up", "w_down", "mlp_post_gain", "norm_a_2", "w_in_a_2", "w_grp_a_2",
        "scale_a_2", "w_out_a_2", "norm_kv_2", "w_k_2", "w_v_2", "norm_b_2", "w_in_b_2", "w_out_b_2", "norm_f_2"]


def shape_constants():
    f = np.float32
    inv_freq = (f(1.0) / (f(10000.0) ** (np.arange(0, P, 2, dtype=f) / f(P)))).astype(f)
    ang = np.arange(TOKENS, dtype=f)[:, None] * inv_freq[None, :]
    cos, sin = np.cos(ang).astype(f), np.sin(ang).astype(f)
    rope = np.stack([cos, -sin, sin], axis=1).reshape(HALVES, P, 3, P // 2).transpose(1, 0, 2, 3)
    q = np.arange(P)[:, None]
    k = np.arange(P)[None, :]
    masks = np.zeros((P, 2, GROUPS, P), f)
    for b, shift in enumerate((P, 0)):
        back = q + shift - k
        for g, d in enumerate(DILATIONS):
            seen = (back >= 0) & (back % d == 0) & (back <= REACH * d)
            masks[:, b, g, :] = np.where(seen, 0.0, MASKED)
    counts = np.zeros((P, len(POOL_WINDOWS), POOL_PAD), f)
    for g, w in enumerate(POOL_WINDOWS):
        counts[:, g, :] = f(1.0) / np.minimum(np.arange(1, POOL_PAD + 1), w).astype(f)
    return {"c_ident": np.eye(P, dtype=f), "c_rope": np.ascontiguousarray(rope),
            "c_masks": masks.reshape(P, 2, GROUPS * P), "c_counts": counts}


def kernel(**inputs):
    import concourse.bacc as bacc
    from concourse.bass_utils import run_bass_kernel_spmd

    nc = bacc.Bacc("TRN2", target_bir_lowering=False, num_devices=1)
    arrays, tensors = {}, {}
    given = {name: np.ascontiguousarray(inputs[name]) for name in _INS}
    given.update(shape_constants())
    for name, a in given.items():
        arrays[f"in_{name}"] = a
        tensors[name] = nc.dram_tensor(f"in_{name}", a.shape, mybir.dt.from_np(a.dtype), kind="ExternalInput").ap()
    tensors["residual"] = nc.dram_tensor("residual", (TOKENS, D), F32).ap()
    out = nc.dram_tensor("out_0", (1, TOKENS, D), F32, kind="ExternalOutput").ap()
    build(nc, tensors, out)
    got = run_bass_kernel_spmd(nc, [arrays], core_ids=[0])
    return got.results[0]["out_0"]
```

```python
from contextlib import ExitStack

import numpy as np

import concourse.bass as bass
from concourse import mybir
from concourse.alu_op_type import AluOpType as ALU

F32 = mybir.dt.float32
F32R = mybir.dt.float32r
ACT = mybir.ActivationFunctionType
AX_X = mybir.AxisListType.X

P = 128
TOKENS = 256
HALVES = TOKENS // P
D = 2048
KT = D // P
D_A = D // 2
TILES_A = D_A // P
D_FF = 4 * D
CONV_A = 3
CONV_B = 31
EPS = 1e-6
HEADS = D // P
GROUPS = 3
DILATIONS = (1, 4, 16)
REACH = 128
SCORE_SCALE = 1.0 / float(P) ** 0.5
POOL_WINDOWS = (2, 4, 8, 16)
POOL_PAD = 16
BANK = 512
UNIT = 1024
RAW_SLOTS = 4
SPLIT_SLOTS = 8
NARROW = 256
WIDE = 512
SUPER = 1024
MASKED = -1e30
ROW_CONV_B = 0
ROW_CONV_A = ROW_CONV_B + CONV_B
ROW_BIAS_B = ROW_CONV_A + CONV_A
ROW_LN_GAIN = ROW_BIAS_B + 1
ROW_LN_BIAS = ROW_LN_GAIN + 1
ROW_SCALE = ROW_LN_BIAS + 1
ROWS = ROW_SCALE + 2


class Signal:

    def __init__(self, sem):
        self.sem = sem
        self.count = 0

    def next(self, by):
        self.count += by
        return (self, self.count)


class Queue:

    def __init__(self, done):
        self.done = done
        self.items = []

    def run(self, make, after=(), signal=None, by=1, silent=False):
        waits = [t for t in after if t is not None]
        signal = None if silent else (signal or self.done)
        token = signal.next(by) if signal is not None else None
        self.items.append((waits, make, signal, by))
        return token

    def emit(self, engine):
        reached = {}
        for waits, make, signal, by in self.items:
            for producer, value in waits:
                if reached.get(producer, 0) < value:
                    engine.wait_ge(producer.sem, value)
                    reached[producer] = value
            if make is None:
                continue
            made = make(engine)
            if signal is not None:
                made.then_inc(signal.sem, by)


class Job:

    def __init__(self, weight, first_tile, tiles, c0, wide):
        self.tiles = tiles
        self.wide = wide
        width = WIDE if wide else NARROW
        self.per_unit = UNIT // width
        self.units = []
        for k in range(first_tile, first_tile + tiles, self.per_unit):
            rows = weight[k * P:(k + self.per_unit) * P, c0:c0 + width]
            self.units.append((rows.rearrange("(k p) n -> p k n", p=P), self.per_unit, width))


def build(nc, t, out):
    ctx = ExitStack()
    with ctx:
        def sb(name, shape, dt=F32):
            return ctx.enter_context(nc.sbuf_tensor(name, shape, dt))

        def signal(name):
            return Signal(ctx.enter_context(nc.semaphore(name)))

        pe = Queue(signal("tensor_done"))
        dve = Queue(signal("vector_done"))
        act = Queue(signal("scalar_done"))
        pool = Queue(signal("gpsimd_done"))
        sp = Queue(None)

        raw = sb("raw_weights", [P, RAW_SLOTS, UNIT])
        high = sb("weights_high", [P, SPLIT_SLOTS, UNIT], F32R)
        low = sb("weights_low", [P, SPLIT_SLOTS, UNIT], F32R)
        act_a = sb("act_a", [P, KT, 2, TOKENS], F32R)
        act_b = sb("act_b", [P, KT, 2, TOKENS], F32R)
        resid = sb("resid", [P, HALVES, D])
        wide_rows = sb("wide_rows", [P, HALVES, D])
        ident = sb("ident", [P, P])
        early = sb("early_tables", [P, TILES_A * ROWS + P])
        feature = early[:, 0:TILES_A * ROWS].rearrange("p (a b) -> p a b", a=TILES_A)
        mean_ones = early[:, TILES_A * ROWS:]
        turned_p_buf = early[:, 0:3 * P]
        rope = sb("rope", [P, 2, TOKENS])
        masks = sb("masks", [P, 2, GROUPS * P], mybir.dt.bfloat16)
        counts = sb("counts", [P, len(POOL_WINDOWS), POOL_PAD])
        eps = sb("eps", [P, 1])
        minus_half = sb("minus_half", [P, 1])
        sumsq = sb("sumsq", [P, HALVES, 8])
        rstd = sb("rstd", [P, HALVES])
        soft = sb("soft", [P, HALVES, 4])
        scratch = sb("scratch", [P, 4096 + P])
        partial = sb("partial", [P, 2, BANK])
        value = sb("value", [P, 2, BANK])

        banks = ctx.enter_context(nc.psum_tensor("job_banks", [P, 4, BANK], F32))
        aux = ctx.enter_context(nc.psum_tensor("aux_banks", [P, 4, BANK], F32))

        raw_ready = [signal(f"raw_ready{i}") for i in range(RAW_SLOTS)]
        const_ready = signal("const_ready")
        ident_ready = signal("ident_ready")
        x_ready = [signal(f"x_ready{i}") for i in range(HALVES)]
        row_ready = [signal(f"row_ready{i}") for i in range(2)]
        spilled = [signal(f"residual_spilled{i}") for i in range(HALVES)]
        reloaded = signal("residual_reloaded")
        stored = signal("output_stored")

        w_in, w_out, w_up, w_down = t["w_in"][0], t["w_out"][0], t["w_up"][0], t["w_down"][0]
        w_in_a, w_grp, w_out_a = t["w_in_a_2"][0], t["w_grp_a_2"][0], t["w_out_a_2"][0]
        w_k, w_v, w_in_b, w_out_b = t["w_k_2"], t["w_v_2"], t["w_in_b_2"][0], t["w_out_b_2"][0]

        def narrow_jobs(weight, tiles, c0, width):
            return [Job(weight, 0, tiles, c, False) for c in range(c0, c0 + width, NARROW)]

        def wide_jobs(weight, first_tile=0, tiles=KT):
            return [Job(weight, first_tile, tiles, c, True) for c in range(0, D, WIDE)]

        pairs = D_A // NARROW
        parts_in = [narrow_jobs(w_in, KT, i * D_A, D_A) for i in range(5)]
        mix_b = [j for i in range(pairs) for j in (parts_in[4][i], parts_in[3][i])]
        mix_a = [j for i in range(pairs) for j in (parts_in[1][i], parts_in[2][i], parts_in[0][i])]
        proj = wide_jobs(w_out)
        supers = D_FF // SUPER
        z_tiles = SUPER // P
        up = [narrow_jobs(w_up, KT, s * SUPER, SUPER) for s in range(supers)]
        down = [wide_jobs(w_down, s * z_tiles, z_tiles) for s in range(supers)]
        pool_gate = narrow_jobs(w_in_a, KT, D, D)
        pool_u = narrow_jobs(w_in_a, KT, 0, D)
        n_pool = len(POOL_WINDOWS)
        group_dim = D // n_pool
        grp = [narrow_jobs(w_grp[g], group_dim // P, 0, group_dim) for g in range(n_pool)]
        proj_a = wide_jobs(w_out_a)
        keys = narrow_jobs(w_k, KT, 0, D)
        vals = wide_jobs(w_v)
        batches = D // NARROW
        by_group = [narrow_jobs(w_in_b, KT, g * D, D) for g in range(GROUPS)]
        queries = [[by_group[g][b] for g in range(GROUPS)] for b in range(batches)]
        gates = narrow_jobs(w_in_b, KT, GROUPS * D, D)
        proj_b = wide_jobs(w_out_b)

        order = mix_b + mix_a + proj + up[0]
        for s in range(1, supers):
            order += up[s] + down[s - 1]
        mlp_from, mlp_to = len(order) - len(up[-1] + down[-1]) * (supers - 1), len(order)
        order += down[-1] + pool_u + pool_gate + [j for g in grp for j in g] + proj_a
        order += keys + vals + [j for b in queries for j in b] + gates + proj_b
        units = [u for j in order for u in j.units]
        convolving = sum(len(j.units) for j in mix_b + mix_a)
        vector_only = range(sum(len(j.units) for j in order[:mlp_from]),
                            sum(len(j.units) for j in order[:mlp_to - 2]))

        loaded, high_done, low_done, released = [], [], [], []

        def load_unit(n):
            src, k, width = units[n]
            slot = n % RAW_SLOTS
            dst = raw[:, slot, :].rearrange("p (k n) -> p k n", k=k)
            free = [high_done[n - RAW_SLOTS], low_done[n - RAW_SLOTS]] if n >= RAW_SLOTS else []
            loaded.append(sp.run(lambda e: e.dma_start(dst, src), free, raw_ready[slot], 16))

        def split_unit(n):
            r, s = n % RAW_SLOTS, n % SPLIT_SLOTS
            free = released[n - SPLIT_SLOTS] if n >= SPLIT_SLOTS else None
            high_done.append(act.run(lambda e: e.activation(high[:, s, :], raw[:, r, :], ACT.Copy),
                                     [loaded[n], free]))
            theirs = n % 3 > 0 if n < convolving else n % 2 == 1 and n not in vector_only
            eng = pool if theirs else dve
            low_done.append(eng.run(lambda e: e.tensor_tensor(low[:, s, :], raw[:, r, :], high[:, s, :].bitcast(F32),
                                                              ALU.subtract), [loaded[n], high_done[n], free]))

        def prepare(n):
            while len(low_done) <= min(n, len(units) - 1):
                while len(loaded) <= min(len(low_done) + RAW_SLOTS - 1, len(units) - 1):
                    load_unit(len(loaded))
                split_unit(len(low_done))

        beside = []

        def step():
            while beside:
                try:
                    next(beside[0])
                    return
                except StopIteration:
                    beside.pop(0)

        def follow(steps):
            next(steps)
            beside.append(steps)

        def finish():
            while beside:
                step()

        at = [0]
        turn = [0]
        bank_free = [()] * 4
        ready = {b: [[[], []] for _ in range(KT)] for b in "ab"}
        act_free = {"a": [None] * KT, "b": [None] * KT}
        bufs = {"a": act_a, "b": act_b}

        def take_units(job):
            n = at[0]
            at[0] += len(job.units)
            return n

        def next_pair():
            turn[0] += 1
            return (turn[0] - 1) % 2

        def free_unit(token):
            released.append(token)
            prepare(len(released) - 1 + SPLIT_SLOTS)
            step()

        def narrow_unit(job, buf, first, pair, n, u, halves):
            s = n % SPLIT_SLOTS
            wh = high[:, s, :].rearrange("p (k n) -> p k n", n=NARROW)
            wl = low[:, s, :].rearrange("p (k n) -> p k n", n=NARROW)
            x, last = bufs[buf], None
            toks = slice(halves[0] * P, (halves[-1] + 1) * P)
            for k in range(job.per_unit):
                kt = u * job.per_unit + k
                for f in range(2):
                    bank = 2 * pair + f
                    cols = slice(f * P, (f + 1) * P)
                    waits = [low_done[n], high_done[n]] + (list(bank_free[bank]) if kt == 0 else [])
                    for h in halves:
                        waits = waits + ready[buf][first + kt][h]
                    o = banks[:, bank, :].rearrange("p (a n) -> p a n", a=2)
                    if len(halves) == 2:
                        o_both, rhs = banks[:, bank, :], x[:, first + kt, :, :].rearrange("p a n -> p (a n)")
                    else:
                        o_both, rhs = o[:, :, toks], x[:, first + kt, :, toks]
                    pe.run(lambda e, o=o_both, l=wh[:, k, cols], r=rhs, a=(kt == 0): e.matmul(
                        o, l, r, start=a, stop=False), waits, silent=True)
                    end = k == job.per_unit - 1 and f == 1
                    last = pe.run(lambda e, o=o[:, 0, toks], l=wl[:, k, cols], r=x[:, first + kt, 0, toks],
                                  z=(kt == job.tiles - 1): e.matmul(o, l, r, start=False, stop=z), silent=not end)
            return last

        def narrow(job, buf, first=0):
            pair, n0 = next_pair(), take_units(job)
            for u in range(len(job.units)):
                last = narrow_unit(job, buf, first, pair, n0 + u, u, (0, 1))
                for k in range(first + u * job.per_unit, first + (u + 1) * job.per_unit):
                    act_free[buf][k] = last
                free_unit(last)
            return pair, last

        def narrow_by_half(two, buf, between):
            where = [(job, next_pair(), take_units(job)) for job in two]
            for job, pair, n0 in where:
                for u in range(len(job.units)):
                    narrow_unit(job, buf, 0, pair, n0 + u, u, (0,))
            between()
            ends = []
            for job, pair, n0 in where:
                for u in range(len(job.units)):
                    last = narrow_unit(job, buf, 0, pair, n0 + u, u, (1,))
                    free_unit(last)
                ends.append((pair, last))
            act_free[buf] = [last] * KT
            return ends

        def wide_unit(job, buf, first, pair, n, u, half, signal_end):
            s = n % SPLIT_SLOTS
            wh = high[:, s, :].rearrange("p (k n) -> p k n", n=WIDE)
            wl = low[:, s, :].rearrange("p (k n) -> p k n", n=WIDE)
            bank = 2 * pair + half
            o, x, last = banks[:, bank, :], bufs[buf], None
            for k in range(job.per_unit):
                kt = u * job.per_unit + k
                toks = slice(half * P, (half + 1) * P)
                xh, xl = x[:, first + kt, 0, toks], x[:, first + kt, 1, toks]
                waits = [low_done[n], high_done[n]] + ready[buf][first + kt][half]
                waits += bank_free[bank] if kt == 0 else ()
                for i, (l, r) in enumerate(((xh, wh[:, k, :]), (xh, wl[:, k, :]), (xl, wh[:, k, :]))):
                    end = signal_end and k == job.per_unit - 1 and i == 2
                    last = pe.run(lambda e, l=l, r=r, a=(kt == 0 and i == 0), z=(kt == job.tiles - 1 and i == 2):
                                  e.matmul(o, l, r, start=a, stop=z), waits if i == 0 else (), silent=not end)
            return last

        def wide(job, buf, take, first=0):
            pair, n0 = next_pair(), take_units(job)
            count = len(job.units)
            for u in range(count):
                ends = [wide_unit(job, buf, first, pair, n0 + u, u, half, half == 1 or u == count - 1)
                        for half in range(HALVES)]
                free_unit(ends[1])
            for kt in range(first, first + job.tiles):
                act_free[buf][kt] = ends[1]
            for half in range(HALVES):
                bank_free[2 * pair + half] = take(half, banks[:, 2 * pair + half, :], ends[half])

        def wide_by_half(jobs, buf, takes, first, after_first):
            where = [(job, next_pair(), take_units(job)) for job in jobs]
            for half in range(HALVES):
                for (job, pair, n0), take in zip(where, takes):
                    for u in range(len(job.units)):
                        last = wide_unit(job, buf, first, pair, n0 + u, u, half, half == 1 or u == len(job.units) - 1)
                        if half == 1:
                            free_unit(last)
                    bank_free[2 * pair + half] = take(half, banks[:, 2 * pair + half, :], last)
                if half == 0:
                    follow(after_first())
            for kt in range(first, first + jobs[0].tiles):
                act_free[buf][kt] = last

        def split_act(buf, kts, halves, src, after, scale=1.0):
            toks = slice(halves[0] * P, (halves[-1] + 1) * P)
            hi, lo = bufs[buf][:, kts, 0, toks], bufs[buf][:, kts, 1, toks]
            free = [act_free[buf][k] for k in range(kts.start, kts.stop)]
            h = act.run(lambda e: e.activation(hi, src, ACT.Copy, scale=scale), after + free)
            if scale == 1.0:
                l = dve.run(lambda e: e.tensor_tensor(lo, src, hi.bitcast(F32), ALU.subtract), after + free + [h])
            else:
                l = dve.run(lambda e: e.scalar_tensor_tensor(lo, src, scale, hi.bitcast(F32), ALU.mult,
                                                             ALU.subtract), after + free + [h])
            for k in range(kts.start, kts.stop):
                for half in halves:
                    ready[buf][k][half] = [h, l]
            return l

        BOTH = (0, 1)
        slot_free = [None, None]
        part_free = [None, None]

        def gather(pair, done):
            ps = banks[:, 2 * pair:2 * pair + 2, :]
            part = partial[:, pair, :].rearrange("p (f n) -> p f n", f=2)
            v = value[:, pair, :].rearrange("p (f n) -> p f n", f=2)
            c = act.run(lambda e: e.activation(part, ps[:, :, TOKENS:2 * TOKENS], ACT.Copy),
                        [done, part_free[pair]])
            s = dve.run(lambda e: e.tensor_tensor(v, ps[:, :, 0:TOKENS], part, ALU.add), [c, slot_free[pair]])
            part_free[pair] = s
            bank_free[2 * pair] = bank_free[2 * pair + 1] = (s,)
            return v, part, s

        aux_turn = [0]
        aux_free = [None] * 4

        def inverse_rms(half, parts, after):
            tot = sumsq[:, half, 7:8]
            a = dve.run(lambda e: e.tensor_reduce(tot, sumsq[:, half, 0:parts], AX_X, ALU.add), after)
            b = dve.run(lambda e: e.tensor_scalar(tot, tot, 1.0 / D, EPS, ALU.mult, ALU.add), [a])
            return pool.run(lambda e: e.tensor_tensor(rstd[:, half:half + 1], tot, minus_half[:, 0:1], ALU.pow),
                            [b, halves_made])

        rows = [scratch[:, 0:D], scratch[:, D:2 * D]]
        row_used = [None, None]
        row_loaded = [None, None]
        PIECES = [slice(c, c + WIDE) for c in range(0, D, WIDE)]

        def load_row(i, src, after, queue=sp):
            row_loaded[i] = queue.run(lambda e: e.dma_start(rows[i], src.partition_broadcast(P)),
                                      after + [row_used[i]], row_ready[i], 16)

        def squares_of(half, c, src, junk, after):
            return act.run(lambda e: e.activation(junk, src, ACT.Square, accum_out=sumsq[:, half, c:c + 1]), after)

        def turned(half, row, buf, r, after, pause):
            h, n = resid[:, half, :], wide_rows[:, half, :]
            scaled = []

            def scale_piece(c):
                scaled.append(dve.run(lambda e: e.scalar_tensor_tensor(
                    n[:, PIECES[c]], h[:, PIECES[c]], rstd[:, half:half + 1], rows[row][:, PIECES[c]],
                    ALU.mult, ALU.mult), [r, row_loaded[row]] + after))
                row_used[row] = scaled[-1]

            for c in range(len(PIECES) if pause else 1):
                scale_piece(c)
            for _ in range(pause):
                yield
            for c in range(len(PIECES)):
                if len(scaled) < len(PIECES):
                    scale_piece(c + 1)
                b = aux_turn[0] % 4
                aux_turn[0] += 1
                for i in range(WIDE // P):
                    k = c * (WIDE // P) + i
                    done = pe.run(lambda e, b=b, i=i, k=k: e.transpose(aux[:, b, i * P:(i + 1) * P],
                                                                       n[:, k * P:(k + 1) * P], ident[:, :]),
                                  [scaled[c], aux_free[b], ident_there], silent=i < WIDE // P - 1)
                src = aux[:, b, :].rearrange("p (k n) -> p k n", n=P)
                kts = slice(c * (WIDE // P), (c + 1) * (WIDE // P))
                aux_free[b] = split_act(buf, kts, (half,), src, [done])
                if pause:
                    yield
            turned_done[half] = done

        turned_done = [None, None]

        ident_there = act.run(lambda e: e.dma_start(ident[:, :], t["c_ident"]), (), ident_ready, 16)
        x_in = t["x"][0].rearrange("(h p) n -> p h n", p=P)
        x_loaded = []
        for i in range(HALVES):
            x_loaded.append(sp.run(lambda e, i=i: e.dma_start(resid[:, i, :], x_in[:, i, :]), (), x_ready[i], 16))
            if i == 0:
                load_row(0, t["mix_pre_gain"][0], [])
        eps_made = dve.run(lambda e: e.memset(eps[:, :], EPS))
        halves_made = pool.run(lambda e: e.memset(minus_half[:, :], -0.5))
        ones_made = dve.run(lambda e: e.memset(mean_ones[:, :], 1.0 / D_A))
        act.run(lambda e: e.activation(rstd[:, 0:1], mean_ones[:, 0:1], ACT.Tanh), [ones_made])
        staging = scratch[0:ROWS, D:D + D_A]
        small = [(staging[ROW_CONV_B:ROW_CONV_B + CONV_B, :], t["conv_b_w"][0]),
                 (staging[ROW_CONV_A:ROW_CONV_A + CONV_A, :], t["conv_a_w"][0]),
                 (staging[ROW_BIAS_B:ROW_BIAS_B + 1, :], t["conv_b_bias"]),
                 (staging[ROW_LN_GAIN:ROW_LN_GAIN + 1, :], t["ln_b_gain"]),
                 (staging[ROW_LN_BIAS:ROW_LN_BIAS + 1, :], t["ln_b_bias"]),
                 (staging[ROW_SCALE:ROW_SCALE + 2, :], t["scale_a_2"][0].rearrange("(a n) -> a n", a=2)),
                 (rope[:, :, :], t["c_rope"]), (masks[:, :, :], t["c_masks"]), (counts[:, :, :], t["c_counts"])]

        def first_norm(half):
            q = squares_of(half, 0, resid[:, half, :], wide_rows[:, half, :], [x_loaded[half]])
            r = inverse_rms(half, 1, [q])
            yield from turned(half, 0, "a", r, [q], 0)

        def run_all(steps):
            for _ in steps:
                pass

        run_all(first_norm(0))
        prepare(SPLIT_SLOTS - 1)
        for dst, src in small:
            consts = sp.run(lambda e, dst=dst, src=src: e.dma_start(dst, src), (), const_ready, 16)

        gpad_n = TOKENS + CONV_B - 1
        gpad = scratch[:, 0:TILES_A * gpad_n].rearrange("p (j n) -> p j n", j=TILES_A)
        o1 = TILES_A * gpad_n
        cvpad = scratch[:, o1:o1 + 2 * (TOKENS + CONV_A - 1)].rearrange("p (f n) -> p f n", f=2)
        o2 = o1 + 2 * (TOKENS + CONV_A - 1)
        conv3 = scratch[:, o2:o2 + BANK].rearrange("p (f n) -> p f n", f=2)
        o3 = o2 + BANK
        gate_tanh = scratch[:, o3:o3 + BANK].rearrange("p (f n) -> p f n", f=2)
        assert o3 + BANK <= 4096
        conv = wide_rows[:, 0, :].rearrange("p (j n) -> p j n", j=TILES_A)
        squares = wide_rows[:, 1, :].rearrange("p (j n) -> p j n", j=TILES_A)

        def column(row, j):
            return feature[:, j, row:row + 1]

        def make_columns():
            for j in range(TILES_A):
                tok = pe.run(lambda e, j=j: e.transpose(aux[:, 3, j * ROWS:(j + 1) * ROWS],
                                                        staging[:, j * P:(j + 1) * P], ident[0:ROWS, 0:ROWS]),
                             [consts, aux_free[3], ident_there], silent=j < TILES_A - 1)
            f = aux[:, 3, 0:TILES_A * ROWS].rearrange("p (a b) -> p a b", a=TILES_A)
            for lo, hi, scale in ((ROW_CONV_B, ROW_CONV_A, 0.5), (ROW_CONV_A, ROW_SCALE, 1.0),
                                  (ROW_SCALE, ROWS, 0.5)):
                got = dve.run(lambda e, lo=lo, hi=hi, scale=scale: e.tensor_scalar(
                    feature[:, :, lo:hi], f[:, :, lo:hi], scale, None, ALU.mult), [tok])
            aux_free[3] = got
            z = dve.run(lambda e: e.memset(gpad[:, :, 0:CONV_B - 1], 0.0), [row_used[0], tok])
            z = dve.run(lambda e: e.memset(cvpad[:, :, 0:CONV_A - 1], 0.0), [z])
            return got, z

        conv_done = [None] * TILES_A
        mixed_done = []
        CONV_STEP = 5

        def convolve(i, after):
            tiles = (2 * i, 2 * i + 1)
            for j in tiles:
                conv_done[j] = dve.run(lambda e, j=j: e.tensor_scalar(
                    conv[:, j, :], gpad[:, j, 0:TOKENS], column(ROW_CONV_B, j), column(ROW_BIAS_B, j),
                    ALU.mult, ALU.add), after + turned_done)
            for k in range(1, CONV_B):
                for j in tiles:
                    if (2 * k + j % 2) % CONV_STEP == 0:
                        yield
                    conv_done[j] = dve.run(lambda e, j=j, k=k: e.scalar_tensor_tensor(
                        conv[:, j, :], gpad[:, j, k:k + TOKENS], column(ROW_CONV_B + k, j), conv[:, j, :],
                        ALU.mult, ALU.add), [conv_done[j]])

        def mean_of(src, after, bank):
            for j in range(TILES_A):
                done = pe.run(lambda e, j=j: e.matmul(aux[:, bank, 0:TOKENS], mean_ones[:, :], src[:, j, :],
                                                      start=j == 0, stop=j == TILES_A - 1),
                              after + [aux_free[bank], ones_made], silent=j < TILES_A - 1)
            return done

        def layer_norm():
            yield
            m = mean_of(conv, conv_done, 0)
            yield
            for j in range(TILES_A):
                d = dve.run(lambda e, j=j: e.tensor_tensor(conv[:, j, :], conv[:, j, :], aux[:, 0, 0:TOKENS],
                                                           ALU.subtract), [m])
            aux_free[0] = d
            sq = act.run(lambda e: e.activation(squares, conv, ACT.Square), [d] + turned_done)
            yield
            yield
            yield
            v = mean_of(squares, [sq], 1)
            yield
            a = act.run(lambda e: e.activation(inv, aux[:, 1, 0:TOKENS], ACT.Sqrt, bias=eps[:, 0:1]),
                        [v, eps_made] + conv_done)
            b = dve.run(lambda e: e.reciprocal(inv, inv), [a])
            aux_free[1] = a
            yield
            for i in range(TILES_A // 2):
                toks = []
                for j in (2 * i, 2 * i + 1):
                    c = dve.run(lambda e, j=j: e.tensor_tensor(conv[:, j, :], conv[:, j, :], inv, ALU.mult), [b])
                    toks.append(dve.run(lambda e, j=j: e.tensor_scalar(
                        conv[:, j, :], conv[:, j, :], column(ROW_LN_GAIN, j), column(ROW_LN_BIAS, j),
                        ALU.mult, ALU.add), [c]))
                two = slice(2 * i, 2 * i + 2)
                s = act.run(lambda e, two=two: e.activation(squares[:, two, :], conv[:, two, :], ACT.Tanh, scale=0.5),
                            toks + [v])
                y = dve.run(lambda e, two=two: e.scalar_tensor_tensor(squares[:, two, :], squares[:, two, :], 1.0,
                                                                      conv[:, two, :], ALU.add, ALU.mult), [s])
                mixed_done.append(split_act("b", slice(TILES_A + 2 * i, TILES_A + 2 * i + 2), BOTH,
                                            squares[:, two, :], [y], 0.5))
                yield

        inv = gpad[:, 0, 0:TOKENS]
        tanh_done, g_done = None, None

        def take_gate(pair, done):
            v, _, s = gather(pair, done)
            sg = act.run(lambda e: e.activation(gate_tanh, v, ACT.Tanh, scale=0.5), [s, g_done, zero_pads])
            slot_free[pair] = sg
            return sg

        def take_val(i, pair, done):
            v, _, s = gather(pair, done)
            dst = gpad[:, 2 * i:2 * i + 2, CONV_B - 1:]
            g = dve.run(lambda e: e.scalar_tensor_tensor(dst, gate_tanh, 1.0, v, ALU.add, ALU.mult),
                        [s, tanh_done, zero_pads])
            slot_free[pair] = g
            beside.append(convolve(i, [g, features]))
            return g

        def second_half_of_x():
            run_all(first_norm(1))

        ends = narrow_by_half(mix_b[0:2], "a", second_half_of_x)
        features, zero_pads = make_columns()
        tanh_done = take_gate(*ends[0])
        g_done = take_val(0, *ends[1])
        for i in range(1, pairs):
            tanh_done = take_gate(*narrow(mix_b[2 * i], "a"))
            g_done = take_val(i, *narrow(mix_b[2 * i + 1], "a"))
        beside.append(layer_norm())

        cv_free = None
        for i in range(pairs):
            c_job, v_job, b_job = mix_a[3 * i:3 * i + 3]
            pair_c, done = narrow(c_job, "a")
            vc, _, sc = gather(pair_c, done)
            cp = act.run(lambda e, vc=vc: e.activation(cvpad[:, :, CONV_A - 1:], vc, ACT.Copy),
                         [sc, zero_pads, cv_free])
            slot_free[pair_c] = cp
            pair, done = narrow(v_job, "a")
            vv, _, s = gather(pair, done)
            cv = dve.run(lambda e, vv=vv: e.tensor_tensor(cvpad[:, :, CONV_A - 1:], cvpad[:, :, CONV_A - 1:], vv,
                                                          ALU.mult), [s, cp])
            slot_free[pair] = cv
            toks = [None, None]
            for k in range(CONV_A):
                for f in range(2):
                    j = 2 * i + f
                    if k == 0:
                        toks[f] = dve.run(lambda e, f=f, j=j: e.tensor_scalar(
                            conv3[:, f, :], cvpad[:, f, 0:TOKENS], column(ROW_CONV_A, j), None, ALU.mult),
                            [cv, cv_free])
                    else:
                        toks[f] = dve.run(lambda e, f=f, j=j, k=k: e.scalar_tensor_tensor(
                            conv3[:, f, :], cvpad[:, f, k:k + TOKENS], column(ROW_CONV_A + k, j), conv3[:, f, :],
                            ALU.mult, ALU.add), [toks[f]])
            pair, done = narrow(b_job, "a")
            vb, _, s = gather(pair, done)
            y = dve.run(lambda e, vb=vb: e.tensor_tensor(conv3, vb, conv3, ALU.mult), [s] + toks)
            slot_free[pair] = y
            cv_free = split_act("b", slice(2 * i, 2 * i + 2), BOTH, conv3, [y])
        finish()

        load_row(0, t["mix_post_gain"][0], [cv_free] + mixed_done)
        load_row(1, t["mlp_pre_gain"][0], [cv_free] + mixed_done)

        def add_normed(half, got, row, buf, pause):
            n, h = wide_rows[:, half, :], resid[:, half, :]
            r = inverse_rms(half, D // WIDE, got)
            sq = []
            for c, cols in enumerate(PIECES):
                a = dve.run(lambda e, cols=cols: e.scalar_tensor_tensor(
                    h[:, cols], n[:, cols], rstd[:, half:half + 1], h[:, cols], ALU.mult, ALU.add), [r])
                sq.append(squares_of(half, c, h[:, cols], n[:, cols], [a]))
            r = inverse_rms(half, D // WIDE, sq)
            yield from turned(half, row, buf, r, sq, pause)

        def take_normed(c, got, wide_free):
            def take(half, ps, done):
                a = dve.run(lambda e: e.tensor_tensor(wide_rows[:, half, PIECES[c]], ps, rows[0][:, PIECES[c]],
                                                      ALU.mult), [done, row_loaded[0]] + wide_free)
                row_used[0] = a
                b = squares_of(half, c, ps, partial[:, half, :], [a, part_free[half]])
                part_free[half] = b
                got[half] += [a, b]
                return a, b
            return take

        got = [[], []]
        takes = [take_normed(c, got, mixed_done) for c in range(len(proj))]
        for job, take in zip(proj[:-1], takes):
            wide(job, "b", take)
        wide_by_half(proj[-1:], "b", takes[-1:], 0, lambda: add_normed(0, got[0], 1, "a", 5))
        finish()

        def second_half_of_norm(got):
            def between():
                run_all(add_normed(1, got[1], 1, "a", 0))
            return between

        def take_up(s, c, pair, done):
            v, _, a = gather(pair, done)
            z = dve.run(lambda e: e.scalar_tensor_tensor(v, v, 0.0, v, ALU.max, ALU.mult), [a])
            k = (s % 2) * z_tiles + 2 * c
            slot_free[pair] = split_act("b", slice(k, k + 2), BOTH, v, [z])

        row_part = [[None] * (D // WIDE) for _ in range(HALVES)]
        got_mlp = [[], []]

        def take_down(s, c):
            def take(half, ps, done):
                dst = wide_rows[:, half, PIECES[c]]
                if s == 0:
                    a = act.run(lambda e: e.activation(dst, ps, ACT.Copy), [done] + turned_done)
                else:
                    a = dve.run(lambda e: e.tensor_tensor(dst, dst, ps, ALU.add), [done, row_part[half][c]])
                row_part[half][c] = a
                if s == supers - 1:
                    b = squares_of(half, c, dst, partial[:, half, :], [a, part_free[half]])
                    part_free[half] = b
                    d = dve.run(lambda e: e.tensor_tensor(dst, dst, rows[0][:, PIECES[c]], ALU.mult),
                                [b, row_loaded[0]])
                    row_used[0] = d
                    got_mlp[half].append(d)
                return (a,)
            return take

        for c, end in enumerate(narrow_by_half(up[0][0:2], "a", second_half_of_norm(got))):
            take_up(0, c, *end)
        load_row(0, t["mlp_post_gain"][0], [])
        load_row(1, t["norm_a_2"][0], [])
        for c in range(2, len(up[0])):
            take_up(0, c, *narrow(up[0][c], "a"))
        for s in range(1, supers):
            for c, job in enumerate(up[s]):
                take_up(s, c, *narrow(job, "a"))
            for c, job in enumerate(down[s - 1]):
                wide(job, "b", take_down(s - 1, c), first=((s - 1) % 2) * z_tiles)
        s, first = supers - 1, ((supers - 1) % 2) * z_tiles
        for c in range(len(down[s]) - 2):
            wide(down[s][c], "b", take_down(s, c), first=first)
        wide_by_half(down[s][-2:], "b", [take_down(s, c) for c in range(len(down[s]) - 2, len(down[s]))], first,
                     lambda: add_normed(0, got_mlp[0], 1, "a", 5))
        finish()

        tiles_g = group_dim // P
        padded = TOKENS + POOL_PAD
        trio = [scratch[:, i * tiles_g * padded:(i + 1) * tiles_g * padded].rearrange("p (j n) -> p j n", j=tiles_g)
                for i in range(3)]
        u_buf, sum_a, sum_b = trio
        jobs_g = group_dim // NARROW

        def window_means(g, window, got_u):
            src, shift, toks, spare = u_buf, 1, got_u, [sum_a, sum_b]
            while shift < window:
                dst = spare[0]
                a = dve.run(lambda e, d=dst, s=src, k=shift: e.tensor_tensor(
                    d[:, :, POOL_PAD:], s[:, :, POOL_PAD:], s[:, :, POOL_PAD - k:POOL_PAD - k + TOKENS], ALU.add),
                    toks + [pool_free])
                spare = [spare[1], dst]
                src, toks, shift = dst, [a], 2 * shift
            other = spare[0]
            late, early = slice(2 * POOL_PAD, None), slice(POOL_PAD, 2 * POOL_PAD)
            a = dve.run(lambda e: e.scalar_tensor_tensor(other[:, :, late], src[:, :, late], 1.0 / window,
                                                         u_buf[:, :, late], ALU.mult, ALU.subtract), toks)
            divisors = counts[:, g, :].unsqueeze(1).to_broadcast([P, tiles_g, POOL_PAD])
            b = dve.run(lambda e: e.tensor_tensor(other[:, :, early], src[:, :, early], divisors, ALU.mult),
                        toks + [consts])
            b = dve.run(lambda e: e.tensor_tensor(other[:, :, early], other[:, :, early], u_buf[:, :, early],
                                                  ALU.subtract), [b])
            return split_act("b", slice(g * tiles_g, (g + 1) * tiles_g), BOTH, other[:, :, POOL_PAD:], [a, b])

        first_ends = narrow_by_half(pool_u[0:2], "a", second_half_of_norm(got_mlp))
        for b in trio:
            zero = dve.run(lambda e, b=b: e.memset(b[:, :, 0:POOL_PAD], 0.0), row_used)
        pool_free = zero
        for g, window in enumerate(POOL_WINDOWS):
            got_u = []
            for i in range(jobs_g):
                pair, done = first_ends.pop(0) if first_ends else narrow(pool_u[g * jobs_g + i], "a")
                v, _, s = gather(pair, done)
                dst = u_buf[:, 2 * i:2 * i + 2, POOL_PAD:]
                a = act.run(lambda e, v=v, dst=dst: e.activation(dst, v, ACT.Copy), [s, pool_free])
                slot_free[pair] = a
                got_u.append(a)
            pool_free = window_means(g, window, got_u)

        silu_gate = wide_rows[:, :, :].rearrange("p h (j n) -> p (h j) n", n=TOKENS)
        gate_done = [None] * KT

        def take_pool_gate(i, pair, done):
            v, _, s = gather(pair, done)
            dst = silu_gate[:, 2 * i:2 * i + 2, :]
            sg = act.run(lambda e: e.activation(dst, v, ACT.Tanh, scale=0.5), [s] + turned_done)
            a = dve.run(lambda e: e.scalar_tensor_tensor(dst, dst, 1.0, v, ALU.add, ALU.mult), [sg])
            slot_free[pair] = a
            gate_done[2 * i] = gate_done[2 * i + 1] = a

        for i, job in enumerate(pool_gate):
            take_pool_gate(i, *narrow(job, "a"))

        for g in range(n_pool):
            for i, job in enumerate(grp[g]):
                pair, done = narrow(job, "b", first=g * tiles_g)
                v, _, s = gather(pair, done)
                k = g * tiles_g + 2 * i
                for f in range(2):
                    j = k + f
                    a = dve.run(lambda e, f=f, j=j, v=v: e.scalar_tensor_tensor(
                        v[:, f, :], v[:, f, :], column(ROW_SCALE + j // TILES_A, j % TILES_A), silu_gate[:, j, :],
                        ALU.mult, ALU.mult), [s, gate_done[j]])
                slot_free[pair] = split_act("a", slice(k, k + 2), BOTH, v, [a])
        gated = slot_free[pair]

        load_row(0, t["norm_kv_2"], [pool_free])
        load_row(1, t["norm_b_2"][0], [pool_free])

        def take_added(c, got, after):
            def take(half, ps, done):
                h = resid[:, half, PIECES[c]]
                a = dve.run(lambda e: e.tensor_tensor(h, h, ps, ALU.add), [done] + after)
                got[half].append(squares_of(half, c, h, partial[:, half, :], [a, part_free[half]]))
                part_free[half] = got[half][-1]
                return (a,)
            return take

        got_a = [[], []]
        norm_a = [None, None]

        def norm_keys(half, pause):
            norm_a[half] = inverse_rms(half, D // WIDE, got_a[half])
            yield from turned(half, 0, "a", norm_a[half], [gated], pause)

        takes = [take_added(c, got_a, []) for c in range(len(proj_a))]
        for job, take in zip(proj_a[:-1], takes):
            wide(job, "a", take)
        wide_by_half(proj_a[-1:], "a", takes[-1:], 0, lambda: norm_keys(0, 2))
        finish()
        resid_dram = t["residual"].rearrange("(h p) n -> p h n", p=P)
        spill = [sp.run(lambda e, i=i: e.dma_start(resid_dram[:, i, :], resid[:, i, :]), got_a[i], spilled[i], 16)
                 for i in range(HALVES)]

        key_t = resid[:, :, :].rearrange("p h (j n) -> p (h j) n", n=TOKENS)
        query_t = scratch[:, 0:2 * GROUPS * 2 * TOKENS].rearrange("p (s g j n) -> p s g j n", s=2, g=GROUPS, j=2)
        mid = P // 2
        cos = rope[:, 0, :].unsqueeze(1).to_broadcast([P, 2, TOKENS])
        sin = rope[:, 1, :].unsqueeze(1).to_broadcast([P, 2, TOKENS])

        def take_rotated(dst, free, pair, done):
            v, part, s = gather(pair, done)
            a = pool.run(lambda e: e.tensor_tensor(part, v, cos, ALU.mult), [s, consts])
            b = dve.run(lambda e: e.tensor_tensor(dst[0:mid], v[mid:P], sin[mid:P], ALU.mult), [s, consts] + free)
            c = dve.run(lambda e: e.tensor_tensor(dst[mid:P], v[0:mid], sin[0:mid], ALU.mult), [s, consts] + free)
            d = dve.run(lambda e: e.tensor_tensor(dst, dst, part, ALU.add), [a, b, c])
            slot_free[pair] = d
            part_free[pair] = d
            return d

        norm_b = {}

        def norm_queries(half):
            yield from turned(half, 1, "b", norm_a[half], [turned_done[half], gated], 1)

        def second_half_of_keys():
            run_all(norm_keys(1, 0))

        ends = narrow_by_half(keys[0:2], "a", second_half_of_keys)
        first_turned = list(turned_done)
        key_done = []
        for half in range(HALVES):
            follow(norm_queries(half))
        for i, end in enumerate(ends):
            key_done.append(take_rotated(key_t[:, 2 * i:2 * i + 2, :], spill + [row_used[1]], *end))
        for i in range(2, len(keys)):
            key_done.append(take_rotated(key_t[:, 2 * i:2 * i + 2, :], spill + [row_used[1]],
                                         *narrow(keys[i], "a")))

        val_done = []

        def take_value(c):
            def take(half, ps, done):
                val_done.append(act.run(lambda e: e.activation(wide_rows[:, half, PIECES[c]], ps, ACT.Copy),
                                        [done] + turned_done))
                return (val_done[-1],)
            return take
        for c, job in enumerate(vals):
            wide(job, "a", take_value(c))

        e0 = 2 * GROUPS * 2 * TOKENS
        e_buf = scratch[:, e0:e0 + 3 * GROUPS * P].rearrange("p (b n) -> p b n", b=3)
        pt_buf = turned_p_buf
        prev = {"e": None, "pt": gated}
        scored_last = [None, None]
        BLOCKS_OF = [slice(0, 1), slice(1, 3)]

        def attend(head, q, q_done):
            scored, weighed = [], []
            for half in range(HALVES):
                for blk in range(half + 1):
                    bank = half + blk
                    for g in range(GROUPS):
                        d = pe.run(lambda e, g=g, bank=bank, half=half, blk=blk: e.matmul(
                            aux[:, bank, g * P:(g + 1) * P], q[:, g, half * P:(half + 1) * P],
                            key_t[:, head, blk * P:(blk + 1) * P], start=True, stop=True),
                            q_done + key_done + [aux_free[bank]], silent=g < GROUPS - 1)
                scored.append(d)
            scored_last[(head // 2) % 2] = scored[1]
            softened = []
            for half, own in enumerate(BLOCKS_OF):
                ps = aux[:, own, 0:GROUPS * P]
                mask = masks[:, 1 - half:2, :]
                st = soft[:, half, :]
                a = dve.run(lambda e, ps=ps, mask=mask, own=own: e.scalar_tensor_tensor(
                    e_buf[:, own, :], ps, SCORE_SCALE, mask, ALU.mult, ALU.add), [scored[half], prev["e"], consts])
                for bank in range(own.start, own.stop):
                    aux_free[bank] = a
                m = dve.run(lambda e, own=own, st=st: e.tensor_reduce(st[:, 0:1], e_buf[:, own, :],
                                                                      mybir.AxisListType.XY, ALU.max), [a])
                m = dve.run(lambda e, st=st: e.tensor_scalar(st[:, 1:2], st[:, 0:1], -1.0, None, ALU.mult), [m])
                softened.append(act.run(lambda e, own=own, st=st: e.activation(
                    e_buf[:, own, :], e_buf[:, own, :], ACT.Exp, bias=st[:, 1:2], accum_out=st[:, 2:3]), [m]))
            e3 = e_buf.rearrange("p b (g n) -> p b g n", g=GROUPS)
            for half, own in enumerate(BLOCKS_OF):
                st = soft[:, half, :]
                r = dve.run(lambda e, st=st: e.reciprocal(st[:, 3:4], st[:, 2:3]), [softened[half]])
                w = e3[:, own, 0, :]
                for g in range(1, GROUPS):
                    r = dve.run(lambda e, w=w, own=own, g=g: e.tensor_tensor(w, w, e3[:, own, g, :], ALU.add), [r])
                weighed.append(act.run(lambda e, w=w, st=st: e.activation(w, w, ACT.Copy, scale=st[:, 3:4]), [r]))
            for _ in range(3):
                yield
            for blk in range(3):
                d = pe.run(lambda e, blk=blk: e.transpose(aux[:, 3, blk * P:(blk + 1) * P], e3[:, blk, 0, :],
                                                          ident[:, :]), weighed + [aux_free[3]], silent=blk < 2)
            prev["e"] = d
            c = act.run(lambda e: e.activation(pt_buf, aux[:, 3, 0:3 * P], ACT.Copy), [d, prev["pt"]])
            aux_free[3] = c
            yield
            yield
            cols = slice(head * P, (head + 1) * P)
            pe.run(lambda e: e.matmul(aux[:, 0, 0:TOKENS], wide_rows[:, 0, cols], pt_buf[:, 0:2 * P],
                                      start=True, stop=False), [c, aux_free[0]] + val_done, silent=True)
            d = pe.run(lambda e: e.matmul(aux[:, 0, P:2 * P], wide_rows[:, 1, cols], pt_buf[:, 2 * P:3 * P],
                                          start=False, stop=True))
            prev["pt"] = d
            aux_free[0] = split_act("a", slice(head, head + 1), BOTH, aux[:, 0:1, 0:TOKENS], [d])
            yield

        for b in range(batches):
            q_done = []
            for g, job in enumerate(queries[b]):
                end = narrow(job, "b")
                if g == 0 and b >= 2:
                    while attended[0] < 2 * (b - 1):
                        step()
                q_done.append(take_rotated(query_t[:, b % 2, g, :, :], [scored_last[b % 2], row_used[1], row_used[0]],
                                           *end))
            if b == 0:
                attended = [0]

            def counted(steps):
                yield from steps
                attended[0] += 1
            for j in range(2):
                beside.append(counted(attend(2 * b + j, query_t[:, b % 2, :, j, :], q_done)))

        for i, job in enumerate(gates):
            pair, done = narrow(job, "b")
            while attended[0] < 2 * (i + 1):
                step()
            v, part, s = gather(pair, done)
            k = slice(2 * i, 2 * i + 2)
            sg = act.run(lambda e, v=v, part=part: e.activation(part, v, ACT.Tanh, scale=0.5), [s])
            a = dve.run(lambda e, v=v, part=part: e.scalar_tensor_tensor(v, part, 1.0, v, ALU.add, ALU.mult), [sg])
            whole = dve.run(lambda e, k=k, part=part: e.tensor_tensor(part, act_a[:, k, 0, :].bitcast(F32),
                                                                      act_a[:, k, 1, :].bitcast(F32), ALU.add),
                            [a] + [x for kt in (2 * i, 2 * i + 1) for x in ready["a"][kt][0]])
            y = dve.run(lambda e, v=v, part=part: e.tensor_tensor(v, v, part, ALU.mult), [whole])
            part_free[pair] = y
            slot_free[pair] = split_act("a", k, BOTH, v, [y], 0.5)
            if i == 1:
                finish()
                load_row(0, t["norm_f_2"], scored_last)
                reload_ = sp.run(lambda e: e.dma_start(resid[:, :, :], resid_dram), spill + scored_last, reloaded, 16)

        out_v = out.rearrange("b (h p) n -> p (b h) n", p=P)
        got_b = [[], []]

        def final_norm(half):
            h, n = resid[:, half, :], wide_rows[:, half, :]
            r = inverse_rms(half, D // WIDE, got_b[half])
            for cols in PIECES:
                s = dve.run(lambda e, cols=cols: e.scalar_tensor_tensor(
                    n[:, cols], h[:, cols], rstd[:, half:half + 1], rows[0][:, cols], ALU.mult, ALU.mult),
                    [r, row_loaded[0], prev["pt"]])
                sp.run(lambda e, cols=cols: e.dma_start(out_v[:, half, cols], n[:, cols]), [s], stored, 16)
            yield

        takes = [take_added(c, got_b, [reload_]) for c in range(len(proj_b))]
        for job, take in zip(proj_b[:-1], takes):
            wide(job, "a", take)
        wide_by_half(proj_b[-1:], "a", takes[-1:], 0, lambda: final_norm(0))
        run_all(final_norm(1))
        for s in (stored, spilled[0], spilled[1]):
            sp.run(None, [(s, s.count)], silent=True)

        block = ctx.enter_context(nc.Block())

        @block.sync
        def _(e):
            sp.emit(e)

        @block.scalar
        def _(e):
            act.emit(e)

        @block.vector
        def _(e):
            dve.emit(e)

        @block.gpsimd
        def _(e):
            pool.emit(e)

        @block.tensor
        def _(e):
            pe.emit(e)


_INS = ["x", "mix_pre_gain", "w_in", "conv_a_w", "conv_b_w", "conv_b_bias", "ln_b_gain", "ln_b_bias", "w_out",
        "mix_post_gain", "mlp_pre_gain", "w_up", "w_down", "mlp_post_gain", "norm_a_2", "w_in_a_2", "w_grp_a_2",
        "scale_a_2", "w_out_a_2", "norm_kv_2", "w_k_2", "w_v_2", "norm_b_2", "w_in_b_2", "w_out_b_2", "norm_f_2"]


def shape_constants():
    f = np.float32
    inv_freq = (f(1.0) / (f(10000.0) ** (np.arange(0, P, 2, dtype=f) / f(P)))).astype(f)
    ang = np.arange(TOKENS, dtype=f)[:, None] * inv_freq[None, :]
    cos, sin = np.cos(ang).astype(f), np.sin(ang).astype(f)
    rope = np.stack([np.concatenate([cos.T, cos.T]), np.concatenate([sin.T, -sin.T])], axis=1)
    q = np.arange(P)[:, None]
    k = np.arange(P)[None, :]
    masks = np.zeros((P, 2, GROUPS, P), f)
    for b, shift in enumerate((P, 0)):
        back = q + shift - k
        for g, d in enumerate(DILATIONS):
            seen = (back >= 0) & (back % d == 0) & (back <= REACH * d)
            masks[:, b, g, :] = np.where(seen, 0.0, MASKED)
    counts = np.zeros((P, len(POOL_WINDOWS), POOL_PAD), f)
    for g, w in enumerate(POOL_WINDOWS):
        counts[:, g, :] = f(1.0) / np.minimum(np.arange(1, POOL_PAD + 1), w).astype(f)
    return {"c_ident": np.eye(P, dtype=f), "c_rope": np.ascontiguousarray(rope),
            "c_masks": masks.reshape(P, 2, GROUPS * P).astype(mybir.dt.np(mybir.dt.bfloat16)), "c_counts": counts}


def kernel(**inputs):
    import concourse.bacc as bacc
    from concourse.bass_utils import run_bass_kernel_spmd

    nc = bacc.Bacc("TRN2", target_bir_lowering=False, num_devices=1)
    arrays, tensors = {}, {}
    given = {name: np.ascontiguousarray(inputs[name]) for name in _INS}
    given.update(shape_constants())
    for name, a in given.items():
        arrays[f"in_{name}"] = a
        tensors[name] = nc.dram_tensor(f"in_{name}", a.shape, mybir.dt.from_np(a.dtype), kind="ExternalInput").ap()
    tensors["residual"] = nc.dram_tensor("residual", (TOKENS, D), F32).ap()
    out = nc.dram_tensor("out_0", (1, TOKENS, D), F32, kind="ExternalOutput").ap()
    build(nc, tensors, out)
    got = run_bass_kernel_spmd(nc, [arrays], core_ids=[0])
    return got.results[0]["out_0"]
```

```python
from contextlib import ExitStack

import numpy as np

import concourse.bass as bass
from concourse import mybir
from concourse.alu_op_type import AluOpType as ALU

F32 = mybir.dt.float32
F32R = mybir.dt.float32r
ACT = mybir.ActivationFunctionType
AX_X = mybir.AxisListType.X

P = 128
TOKENS = 256
HALVES = TOKENS // P
D = 2048
KT = D // P
D_A = D // 2
TILES_A = D_A // P
D_FF = 4 * D
CONV_A = 3
CONV_B = 31
EPS = 1e-6
HEADS = D // P
GROUPS = 3
DILATIONS = (1, 4, 16)
REACH = 128
SCORE_SCALE = 1.0 / float(P) ** 0.5
POOL_WINDOWS = (2, 4, 8, 16)
POOL_PAD = 16
BANK = 512
UNIT = 1024
RAW_SLOTS = 4
SPLIT_SLOTS = 8
NARROW = 256
WIDE = 512
SUPER = 1024
EARLY = 3
LATE = 1
MASKED = -1e30
ROW_CONV_B = 0
ROW_CONV_A = ROW_CONV_B + CONV_B
ROW_BIAS_B = ROW_CONV_A + CONV_A
ROW_LN_GAIN = ROW_BIAS_B + 1
ROW_LN_BIAS = ROW_LN_GAIN + 1
ROW_SCALE = ROW_LN_BIAS + 1
ROWS = ROW_SCALE + 2


class Signal:

    def __init__(self, sem):
        self.sem = sem
        self.count = 0

    def next(self, by):
        self.count += by
        return (self, self.count)


class Queue:

    def __init__(self, done):
        self.done = done
        self.items = []

    def run(self, make, after=(), signal=None, by=1, silent=False):
        waits = [t for t in after if t is not None]
        signal = None if silent else (signal or self.done)
        token = signal.next(by) if signal is not None else None
        self.items.append((waits, make, signal, by))
        return token

    def emit(self, engine):
        reached = {}
        for waits, make, signal, by in self.items:
            for producer, value in waits:
                if reached.get(producer, 0) < value:
                    engine.wait_ge(producer.sem, value)
                    reached[producer] = value
            if make is None:
                continue
            made = make(engine)
            if signal is not None:
                made.then_inc(signal.sem, by)


class Job:

    def __init__(self, weight, first_tile, tiles, c0, wide):
        self.tiles = tiles
        self.wide = wide
        width = WIDE if wide else NARROW
        self.per_unit = UNIT // width
        self.units = []
        for k in range(first_tile, first_tile + tiles, self.per_unit):
            rows = weight[k * P:(k + self.per_unit) * P, c0:c0 + width]
            self.units.append((rows.rearrange("(k p) n -> p k n", p=P), self.per_unit, width))


def build(nc, t, out):
    ctx = ExitStack()
    with ctx:
        def sb(name, shape, dt=F32):
            return ctx.enter_context(nc.sbuf_tensor(name, shape, dt))

        def signal(name):
            return Signal(ctx.enter_context(nc.semaphore(name)))

        pe = Queue(signal("tensor_done"))
        dve = Queue(signal("vector_done"))
        act = Queue(signal("scalar_done"))
        pool = Queue(signal("gpsimd_done"))
        sp = Queue(None)

        raw = sb("raw_weights", [P, RAW_SLOTS, UNIT])
        high = sb("weights_high", [P, SPLIT_SLOTS, UNIT], F32R)
        low = sb("weights_low", [P, SPLIT_SLOTS, UNIT], F32R)
        act_a = sb("act_a", [P, KT, 2, TOKENS], F32R)
        act_b = sb("act_b", [P, KT, 2, TOKENS], F32R)
        resid = sb("resid", [P, HALVES, D])
        wide_rows = sb("wide_rows", [P, HALVES, D])
        ident = sb("ident", [P, P])
        early = sb("early_tables", [P, TILES_A * ROWS + P])
        feature = early[:, 0:TILES_A * ROWS].rearrange("p (a b) -> p a b", a=TILES_A)
        mean_ones = early[:, TILES_A * ROWS:]
        turned_p_buf = early[:, 0:3 * P]
        rope = sb("rope", [P, 2, TOKENS])
        masks = sb("masks", [P, 2, GROUPS * P], mybir.dt.bfloat16)
        counts = sb("counts", [P, len(POOL_WINDOWS), POOL_PAD])
        eps = sb("eps", [P, 1])
        minus_half = sb("minus_half", [P, 1])
        sumsq = sb("sumsq", [P, HALVES, 8])
        rstd = sb("rstd", [P, HALVES])
        soft = sb("soft", [P, HALVES, 4])
        scratch = sb("scratch", [P, 4096 + P])
        partial = sb("partial", [P, 2, BANK])
        value = sb("value", [P, 2, BANK])

        banks = ctx.enter_context(nc.psum_tensor("job_banks", [P, 4, BANK], F32))
        aux = ctx.enter_context(nc.psum_tensor("aux_banks", [P, 4, BANK], F32))

        raw_ready = [signal(f"raw_ready{i}") for i in range(RAW_SLOTS)]
        vectors_ready = signal("vectors_ready")
        const_ready = signal("const_ready")
        ident_ready = signal("ident_ready")
        x_ready = [signal(f"x_ready{i}") for i in range(HALVES)]
        row_ready = [signal(f"row_ready{i}") for i in range(2)]
        spilled = [signal(f"residual_spilled{i}") for i in range(HALVES)]
        reloaded = signal("residual_reloaded")
        stored = signal("output_stored")

        w_in, w_out, w_up, w_down = t["w_in"][0], t["w_out"][0], t["w_up"][0], t["w_down"][0]
        w_in_a, w_grp, w_out_a = t["w_in_a_2"][0], t["w_grp_a_2"][0], t["w_out_a_2"][0]
        w_k, w_v, w_in_b, w_out_b = t["w_k_2"], t["w_v_2"], t["w_in_b_2"][0], t["w_out_b_2"][0]

        def narrow_jobs(weight, tiles, c0, width):
            return [Job(weight, 0, tiles, c, False) for c in range(c0, c0 + width, NARROW)]

        def wide_jobs(weight, first_tile=0, tiles=KT):
            return [Job(weight, first_tile, tiles, c, True) for c in range(0, D, WIDE)]

        pairs = D_A // NARROW
        parts_in = [narrow_jobs(w_in, KT, i * D_A, D_A) for i in range(5)]
        mix_b = [j for i in range(pairs) for j in (parts_in[4][i], parts_in[3][i])]
        mix_a = [j for i in range(pairs) for j in (parts_in[1][i], parts_in[2][i], parts_in[0][i])]
        early_proj = [Job(w_out, k, TILES_A, c * WIDE, True) for k in (0, TILES_A) for c in range(EARLY)]
        proj = wide_jobs(w_out)[EARLY:]
        supers = D_FF // SUPER
        z_tiles = SUPER // P
        up = [narrow_jobs(w_up, KT, s * SUPER, SUPER) for s in range(supers)]
        down = [wide_jobs(w_down, s * z_tiles, z_tiles) for s in range(supers)]
        pool_gate = narrow_jobs(w_in_a, KT, D, D)
        pool_u = narrow_jobs(w_in_a, KT, 0, D)
        n_pool = len(POOL_WINDOWS)
        group_dim = D // n_pool
        grp = [narrow_jobs(w_grp[g], group_dim // P, 0, group_dim) for g in range(n_pool)]
        proj_a = wide_jobs(w_out_a)
        keys = narrow_jobs(w_k, KT, 0, D)
        vals = wide_jobs(w_v)
        batches = D // NARROW
        by_group = [narrow_jobs(w_in_b, KT, g * D, D) for g in range(GROUPS)]
        queries = [[by_group[g][b] for g in range(GROUPS)] for b in range(batches)]
        gates = narrow_jobs(w_in_b, KT, GROUPS * D, D)
        proj_b = wide_jobs(w_out_b)

        order = mix_b + mix_a + early_proj + proj + up[0]
        for s in range(1, supers):
            order += up[s] + down[s - 1]
        mlp_from, mlp_to = len(order) - len(up[-1] + down[-1]) * (supers - 1), len(order)
        order += down[-1] + pool_u + pool_gate + [j for g in grp for j in g] + proj_a
        order += keys + vals + [j for b in queries for j in b] + gates + proj_b
        units = [u for j in order for u in j.units]
        convolving = sum(len(j.units) for j in mix_b + mix_a)
        vector_only = range(sum(len(j.units) for j in order[:mlp_from]),
                            sum(len(j.units) for j in order[:mlp_to - 2]))
        grouped = range(sum(len(j.units) for j in order[:order.index(grp[0][0])]),
                        sum(len(j.units) for j in order[:order.index(proj_a[0])]))

        loaded, high_done, low_done, released = [], [], [], []

        def load_unit(n):
            src, k, width = units[n]
            slot = n % RAW_SLOTS
            dst = raw[:, slot, :].rearrange("p (k n) -> p k n", k=k)
            free = [high_done[n - RAW_SLOTS]] + low_done[n - RAW_SLOTS] if n >= RAW_SLOTS else []
            loaded.append(sp.run(lambda e: e.dma_start(dst, src), free, raw_ready[slot], 16))

        def split_unit(n):
            r, s = n % RAW_SLOTS, n % SPLIT_SLOTS
            free = released[n - SPLIT_SLOTS] if n >= SPLIT_SLOTS else None
            high_done.append(act.run(lambda e: e.activation(high[:, s, :], raw[:, r, :], ACT.Copy),
                                     [loaded[n], free]))
            cut = UNIT // 2
            if n < convolving:
                cut = UNIT // 8
            elif n in grouped:
                cut = UNIT // 4
            elif n in vector_only:
                cut = UNIT
            lows = []
            for eng, cols in ((dve, slice(0, cut)), (pool, slice(cut, UNIT))):
                if cols.start < cols.stop:
                    lows.append(eng.run(lambda e, cols=cols: e.tensor_tensor(
                        low[:, s, cols], raw[:, r, cols], high[:, s, cols].bitcast(F32), ALU.subtract),
                        [loaded[n], high_done[n], free]))
            low_done.append(lows)

        def prepare(n):
            while len(low_done) <= min(n, len(units) - 1):
                while len(loaded) <= min(len(low_done) + RAW_SLOTS - 1, len(units) - 1):
                    load_unit(len(loaded))
                split_unit(len(low_done))

        beside = []

        def step():
            while beside:
                try:
                    next(beside[0])
                    return
                except StopIteration:
                    beside.pop(0)

        def follow(steps):
            next(steps)
            beside.append(steps)

        def finish():
            while beside:
                step()

        at = [0]
        turn = [0]
        bank_free = [()] * 6
        ready = {b: [[[], []] for _ in range(KT)] for b in "ab"}
        act_free = {"a": [None] * KT, "b": [None] * KT}
        bufs = {"a": act_a, "b": act_b}

        def take_units(job):
            n = at[0]
            at[0] += len(job.units)
            return n

        def next_pair():
            turn[0] += 1
            return (turn[0] - 1) % 2

        def free_unit(token):
            released.append(token)
            step()
            prepare(len(released) - 1 + SPLIT_SLOTS)

        def narrow_unit(job, buf, first, pair, n, u, halves, low_halves=None):
            s = n % SPLIT_SLOTS
            wh = high[:, s, :].rearrange("p (k n) -> p k n", n=NARROW)
            wl = low[:, s, :].rearrange("p (k n) -> p k n", n=NARROW)
            x, last = bufs[buf], None
            low_halves = halves if low_halves is None else low_halves
            toks = slice(halves[0] * P, (halves[-1] + 1) * P)
            low_toks = slice(low_halves[0] * P, (low_halves[-1] + 1) * P) if low_halves else None
            for k in range(job.per_unit):
                kt = u * job.per_unit + k
                for f in range(2):
                    bank = 2 * pair + f
                    cols = slice(f * P, (f + 1) * P)
                    waits = low_done[n] + (list(bank_free[bank]) if kt == 0 else [])
                    for h in sorted(set(halves) | set(low_halves)):
                        waits = waits + ready[buf][first + kt][h]
                    o = banks[:, bank, :].rearrange("p (a n) -> p a n", a=2)
                    if len(halves) == 2:
                        o_both, rhs = banks[:, bank, :], x[:, first + kt, :, :].rearrange("p a n -> p (a n)")
                    else:
                        o_both, rhs = o[:, :, toks], x[:, first + kt, :, toks]
                    pe.run(lambda e, o=o_both, l=wh[:, k, cols], r=rhs, a=(kt == 0 and halves[0] == 0): e.matmul(
                        o, l, r, start=a, stop=False), waits, silent=True)
                    end = k == job.per_unit - 1 and f == 1
                    if low_halves:
                        last = pe.run(lambda e, o=o[:, 0, low_toks], l=wl[:, k, cols], r=x[:, first + kt, 0, low_toks],
                                      z=(kt == job.tiles - 1): e.matmul(o, l, r, start=False, stop=z), silent=not end)
            return last

        def narrow(job, buf, first=0):
            pair, n0 = next_pair(), take_units(job)
            for u in range(len(job.units)):
                last = narrow_unit(job, buf, first, pair, n0 + u, u, (0, 1))
                for k in range(first + u * job.per_unit, first + (u + 1) * job.per_unit):
                    act_free[buf][k] = last
                free_unit(last)
            return pair, last

        def narrow_by_half(two, buf, between, takes):
            where = [(job, next_pair(), take_units(job)) for job in two]
            late = lambda job, u: u >= len(job.units) - LATE
            for job, pair, n0 in where:
                for u in range(len(job.units)):
                    narrow_unit(job, buf, 0, pair, n0 + u, u, (0,), () if late(job, u) else (0,))
            between()
            for (job, pair, n0), take in zip(where, takes):
                for u in range(len(job.units)):
                    last = narrow_unit(job, buf, 0, pair, n0 + u, u, (1,), BOTH if late(job, u) else (1,))
                    free_unit(last)
                take(pair, last)
            act_free[buf] = [last] * KT

        def bank_at(bank):
            return banks[:, bank, :] if bank < 4 else aux[:, bank - 2, :]

        def wide_unit(job, buf, first, pair, n, u, half, signal_end, opens=True, closes=True):
            s = n % SPLIT_SLOTS
            wh = high[:, s, :].rearrange("p (k n) -> p k n", n=WIDE)
            wl = low[:, s, :].rearrange("p (k n) -> p k n", n=WIDE)
            bank = 2 * pair + half
            o, x, last = bank_at(bank), bufs[buf], None
            for k in range(job.per_unit):
                kt = u * job.per_unit + k
                toks = slice(half * P, (half + 1) * P)
                xh, xl = x[:, first + kt, 0, toks], x[:, first + kt, 1, toks]
                waits = low_done[n] + ready[buf][first + kt][half]
                waits += bank_free[bank] if kt == 0 and opens else ()
                for i, (l, r) in enumerate(((xh, wh[:, k, :]), (xh, wl[:, k, :]), (xl, wh[:, k, :]))):
                    end = signal_end and k == job.per_unit - 1 and i == 2
                    last = pe.run(lambda e, l=l, r=r, a=(opens and kt == 0 and i == 0),
                                  z=(closes and kt == job.tiles - 1 and i == 2): e.matmul(o, l, r, start=a, stop=z),
                                  waits if i == 0 else (), silent=not end)
            return last

        def wide(job, buf, take, first=0):
            pair, n0 = next_pair(), take_units(job)
            count = len(job.units)
            for u in range(count):
                ends = [wide_unit(job, buf, first, pair, n0 + u, u, half, half == 1 or u == count - 1)
                        for half in range(HALVES)]
                free_unit(ends[1])
            for kt in range(first, first + job.tiles):
                act_free[buf][kt] = ends[1]
            for half in range(HALVES):
                bank_free[2 * pair + half] = take(half, banks[:, 2 * pair + half, :], ends[half])

        def wide_in_two(begun, more, buf, takes, between):
            where = [next_pair(), next_pair(), 2]
            bank_free[4:6] = [(aux_free[2],), (aux_free[3],)]
            for jobs, opens in ((begun, True), (more, False)):
                for job, pair, take in zip(jobs, where, takes):
                    first = 0 if opens else begun[0].tiles
                    n0, count = take_units(job), len(job.units)
                    for u in range(count):
                        ends = [wide_unit(job, buf, first, pair, n0 + u, u, half, half == 1 or u == count - 1,
                                          opens, not opens) for half in range(HALVES)]
                        free_unit(ends[1])
                    for kt in range(first, first + job.tiles):
                        act_free[buf][kt] = ends[1]
                    if not opens:
                        for half in range(HALVES):
                            bank_free[2 * pair + half] = take(half, bank_at(2 * pair + half), ends[half])
                if opens:
                    between()
            aux_free[2], aux_free[3] = bank_free[4][-1], bank_free[5][-1]

        def wide_by_half(jobs, buf, takes, first, after_first):
            where = [(job, next_pair(), take_units(job)) for job in jobs]
            for half in range(HALVES):
                for (job, pair, n0), take in zip(where, takes):
                    for u in range(len(job.units)):
                        last = wide_unit(job, buf, first, pair, n0 + u, u, half, half == 1 or u == len(job.units) - 1)
                        if half == 1:
                            free_unit(last)
                    bank_free[2 * pair + half] = take(half, banks[:, 2 * pair + half, :], last)
                if half == 0:
                    follow(after_first())
            for kt in range(first, first + jobs[0].tiles):
                act_free[buf][kt] = last

        def split_act(buf, kts, halves, src, after, scale=1.0):
            toks = slice(halves[0] * P, (halves[-1] + 1) * P)
            hi, lo = bufs[buf][:, kts, 0, toks], bufs[buf][:, kts, 1, toks]
            free = [act_free[buf][k] for k in range(kts.start, kts.stop)]
            h = act.run(lambda e: e.activation(hi, src, ACT.Copy, scale=scale), after + free)
            if scale == 1.0:
                l = dve.run(lambda e: e.tensor_tensor(lo, src, hi.bitcast(F32), ALU.subtract), after + free + [h])
            else:
                l = dve.run(lambda e: e.scalar_tensor_tensor(lo, src, scale, hi.bitcast(F32), ALU.mult,
                                                             ALU.subtract), after + free + [h])
            for k in range(kts.start, kts.stop):
                for half in halves:
                    ready[buf][k][half] = [h, l]
            return l

        BOTH = (0, 1)
        slot_free = [None, None]
        part_free = [None, None]

        def gather(pair, done):
            ps = banks[:, 2 * pair:2 * pair + 2, :]
            part = partial[:, pair, :].rearrange("p (f n) -> p f n", f=2)
            v = value[:, pair, :].rearrange("p (f n) -> p f n", f=2)
            c = act.run(lambda e: e.activation(part, ps[:, :, TOKENS:2 * TOKENS], ACT.Copy),
                        [done, part_free[pair]])
            s = dve.run(lambda e: e.tensor_tensor(v, ps[:, :, 0:TOKENS], part, ALU.add), [c, slot_free[pair]])
            part_free[pair] = s
            bank_free[2 * pair] = bank_free[2 * pair + 1] = (s,)
            return v, part, s

        aux_turn = [0]
        aux_free = [None] * 4

        def inverse_rms(half, parts, after):
            tot = sumsq[:, half, 7:8]
            a = dve.run(lambda e: e.tensor_reduce(tot, sumsq[:, half, 0:parts], AX_X, ALU.add), after)
            b = dve.run(lambda e: e.tensor_scalar(tot, tot, 1.0 / D, EPS, ALU.mult, ALU.add), [a])
            return pool.run(lambda e: e.tensor_tensor(rstd[:, half:half + 1], tot, minus_half[:, 0:1], ALU.pow),
                            [b, halves_made])

        rows = [scratch[:, 0:D], scratch[:, D:2 * D]]
        row_used = [None, None]
        row_loaded = [None, None]
        PIECES = [slice(c, c + WIDE) for c in range(0, D, WIDE)]

        def load_row(i, src, after, queue=sp):
            row_loaded[i] = queue.run(lambda e: e.dma_start(rows[i], src.partition_broadcast(P)),
                                      after + [row_used[i]], row_ready[i], 16)

        def squares_of(half, c, src, junk, after):
            return act.run(lambda e: e.activation(junk, src, ACT.Square, accum_out=sumsq[:, half, c:c + 1]), after)

        def turned(half, row, buf, r, after, pause, each=1):
            h, n = resid[:, half, :], wide_rows[:, half, :]
            scaled = []

            def scale_piece(c):
                scaled.append(dve.run(lambda e: e.scalar_tensor_tensor(
                    n[:, PIECES[c]], h[:, PIECES[c]], rstd[:, half:half + 1], rows[row][:, PIECES[c]],
                    ALU.mult, ALU.mult), [r, row_loaded[row]] + after))
                row_used[row] = scaled[-1]

            for c in range(len(PIECES)):
                scale_piece(c)
            for _ in range(pause):
                yield
            for c in range(len(PIECES)):
                b = aux_turn[0] % 4
                aux_turn[0] += 1
                for i in range(WIDE // P):
                    k = c * (WIDE // P) + i
                    done = pe.run(lambda e, b=b, i=i, k=k: e.transpose(aux[:, b, i * P:(i + 1) * P],
                                                                       n[:, k * P:(k + 1) * P], ident[:, :]),
                                  [scaled[c], aux_free[b], ident_there], silent=i < WIDE // P - 1)
                src = aux[:, b, :].rearrange("p (k n) -> p k n", n=P)
                kts = slice(c * (WIDE // P), (c + 1) * (WIDE // P))
                aux_free[b] = split_act(buf, kts, (half,), src, [done])
                if pause and (c + 1) % each == 0:
                    yield
            turned_done[half] = done

        turned_done = [None, None]

        ident_there = act.run(lambda e: e.dma_start(ident[:, :], t["c_ident"]), (), ident_ready, 16)
        x_in = t["x"][0].rearrange("(h p) n -> p h n", p=P)
        x_loaded = []
        for i in range(HALVES):
            x_loaded.append(sp.run(lambda e, i=i: e.dma_start(resid[:, i, :], x_in[:, i, :]), (), x_ready[i], 16))
            if i == 0:
                load_row(0, t["mix_pre_gain"][0], [])
                load_unit(0)
                load_unit(1)
        eps_made = dve.run(lambda e: e.memset(eps[:, :], EPS))
        halves_made = pool.run(lambda e: e.memset(minus_half[:, :], -0.5))
        ones_made = dve.run(lambda e: e.memset(mean_ones[:, :], 1.0 / D_A))
        act.run(lambda e: e.activation(rstd[:, 0:1], mean_ones[:, 0:1], ACT.Tanh), [ones_made])
        staging = scratch[0:ROWS, D:D + D_A]
        small = [(staging[ROW_CONV_B:ROW_CONV_B + CONV_B, :], t["conv_b_w"][0]),
                 (staging[ROW_CONV_A:ROW_CONV_A + CONV_A, :], t["conv_a_w"][0]),
                 (staging[ROW_BIAS_B:ROW_BIAS_B + 1, :], t["conv_b_bias"]),
                 (staging[ROW_LN_GAIN:ROW_LN_GAIN + 1, :], t["ln_b_gain"]),
                 (staging[ROW_LN_BIAS:ROW_LN_BIAS + 1, :], t["ln_b_bias"]),
                 (staging[ROW_SCALE:ROW_SCALE + 2, :], t["scale_a_2"][0].rearrange("(a n) -> a n", a=2))]
        for dst, src in small:
            vectors_there = act.run(lambda e, dst=dst, src=src: e.dma_start(dst, src), (), vectors_ready, 16)

        def first_norm(half, pause):
            q = [squares_of(half, c, resid[:, half, cols], wide_rows[:, half, cols], [x_loaded[half]])
                 for c, cols in enumerate(PIECES)]
            r = inverse_rms(half, len(PIECES), q)
            yield from turned(half, 0, "a", r, q, pause)

        def run_all(steps):
            for _ in steps:
                pass

        for n, _ in enumerate(first_norm(0, 1)):
            if n > 0:
                prepare(n - 1)
        prepare(SPLIT_SLOTS - 1)

        gpad_n = TOKENS + CONV_B - 1
        gpad = scratch[:, 0:TILES_A * gpad_n].rearrange("p (j n) -> p j n", j=TILES_A)
        o1 = TILES_A * gpad_n
        cvpad = scratch[:, o1:o1 + 2 * (TOKENS + CONV_A - 1)].rearrange("p (f n) -> p f n", f=2)
        o2 = o1 + 2 * (TOKENS + CONV_A - 1)
        conv3 = scratch[:, o2:o2 + BANK].rearrange("p (f n) -> p f n", f=2)
        o3 = o2 + BANK
        gate_tanh = scratch[:, o3:o3 + BANK].rearrange("p (f n) -> p f n", f=2)
        assert o3 + BANK <= 4096
        conv = wide_rows[:, 0, :].rearrange("p (j n) -> p j n", j=TILES_A)
        squares = wide_rows[:, 1, :].rearrange("p (j n) -> p j n", j=TILES_A)

        def column(row, j):
            return feature[:, j, row:row + 1]

        def make_columns():
            for j in range(TILES_A):
                tok = pe.run(lambda e, j=j: e.transpose(aux[:, 3, j * ROWS:(j + 1) * ROWS],
                                                        staging[:, j * P:(j + 1) * P], ident[0:ROWS, 0:ROWS]),
                             [vectors_there, aux_free[3], ident_there], silent=j < TILES_A - 1)
            f = aux[:, 3, 0:TILES_A * ROWS].rearrange("p (a b) -> p a b", a=TILES_A)
            for lo, hi, scale in ((ROW_CONV_B, ROW_CONV_A, 0.5), (ROW_CONV_A, ROW_SCALE, 1.0),
                                  (ROW_SCALE, ROWS, 0.5)):
                got = dve.run(lambda e, lo=lo, hi=hi, scale=scale: e.tensor_scalar(
                    feature[:, :, lo:hi], f[:, :, lo:hi], scale, None, ALU.mult), [tok])
            aux_free[3] = got
            z = dve.run(lambda e: e.memset(gpad[:, :, 0:CONV_B - 1], 0.0), [row_used[0], tok])
            z = dve.run(lambda e: e.memset(cvpad[:, :, 0:CONV_A - 1], 0.0), [z])
            return got, z

        conv_done = [None] * TILES_A
        mixed_done = []
        CONV_STEP = 5

        def convolve(i, after):
            tiles = (2 * i, 2 * i + 1)
            for j in tiles:
                conv_done[j] = dve.run(lambda e, j=j: e.tensor_scalar(
                    conv[:, j, :], gpad[:, j, 0:TOKENS], column(ROW_CONV_B, j), column(ROW_BIAS_B, j),
                    ALU.mult, ALU.add), after + turned_done)
            for k in range(1, CONV_B):
                for j in tiles:
                    if (2 * k + j % 2) % CONV_STEP == 0:
                        yield
                    conv_done[j] = dve.run(lambda e, j=j, k=k: e.scalar_tensor_tensor(
                        conv[:, j, :], gpad[:, j, k:k + TOKENS], column(ROW_CONV_B + k, j), conv[:, j, :],
                        ALU.mult, ALU.add), [conv_done[j]])

        def mean_of(src, after, bank):
            for j in range(TILES_A):
                done = pe.run(lambda e, j=j: e.matmul(aux[:, bank, 0:TOKENS], mean_ones[:, :], src[:, j, :],
                                                      start=j == 0, stop=j == TILES_A - 1),
                              after + [aux_free[bank], ones_made], silent=j < TILES_A - 1)
            return done

        def layer_norm():
            for _ in range(3):
                yield
            m = mean_of(conv, conv_done, 0)
            yield
            for j in range(TILES_A):
                d = dve.run(lambda e, j=j: e.tensor_tensor(conv[:, j, :], conv[:, j, :], aux[:, 0, 0:TOKENS],
                                                           ALU.subtract), [m])
            aux_free[0] = d
            sq = act.run(lambda e: e.activation(squares, conv, ACT.Square), [d] + turned_done)
            yield
            yield
            yield
            v = mean_of(squares, [sq], 1)
            yield
            a = act.run(lambda e: e.activation(inv, aux[:, 1, 0:TOKENS], ACT.Sqrt, bias=eps[:, 0:1]),
                        [v, eps_made] + conv_done)
            b = dve.run(lambda e: e.reciprocal(inv, inv), [a])
            aux_free[1] = a
            yield
            for i in range(TILES_A // 2):
                toks = []
                for j in (2 * i, 2 * i + 1):
                    c = dve.run(lambda e, j=j: e.tensor_tensor(conv[:, j, :], conv[:, j, :], inv, ALU.mult), [b])
                    toks.append(dve.run(lambda e, j=j: e.tensor_scalar(
                        conv[:, j, :], conv[:, j, :], column(ROW_LN_GAIN, j), column(ROW_LN_BIAS, j),
                        ALU.mult, ALU.add), [c]))
                two = slice(2 * i, 2 * i + 2)
                s = act.run(lambda e, two=two: e.activation(squares[:, two, :], conv[:, two, :], ACT.Tanh, scale=0.5),
                            toks + [v])
                y = dve.run(lambda e, two=two: e.scalar_tensor_tensor(squares[:, two, :], squares[:, two, :], 1.0,
                                                                      conv[:, two, :], ALU.add, ALU.mult), [s])
                mixed_done.append(split_act("b", slice(TILES_A + 2 * i, TILES_A + 2 * i + 2), BOTH,
                                            squares[:, two, :], [y], 0.5))
                yield

        inv = gpad[:, 0, 0:TOKENS]
        features, zero_pads, tanh_done, g_done = None, None, None, None

        def take_gate(pair, done):
            v, _, s = gather(pair, done)
            sg = act.run(lambda e: e.activation(gate_tanh, v, ACT.Tanh, scale=0.5), [s, g_done, zero_pads])
            slot_free[pair] = sg
            return sg

        def take_val(i, pair, done):
            v, _, s = gather(pair, done)
            dst = gpad[:, 2 * i:2 * i + 2, CONV_B - 1:]
            g = dve.run(lambda e: e.scalar_tensor_tensor(dst, gate_tanh, 1.0, v, ALU.add, ALU.mult),
                        [s, tanh_done, zero_pads])
            slot_free[pair] = g
            beside.append(convolve(i, [g, features]))
            return g

        def second_half_of_x():
            run_all(first_norm(1, 0))

        def take_first_gate(pair, done):
            nonlocal features, zero_pads, tanh_done
            features, zero_pads = make_columns()
            tanh_done = take_gate(pair, done)

        def take_first_val(pair, done):
            nonlocal g_done
            g_done = take_val(0, pair, done)

        narrow_by_half(mix_b[0:2], "a", second_half_of_x, [take_first_gate, take_first_val])
        for i in range(1, pairs):
            tanh_done = take_gate(*narrow(mix_b[2 * i], "a"))
            g_done = take_val(i, *narrow(mix_b[2 * i + 1], "a"))
        beside.append(layer_norm())

        cv_free = None
        for i in range(pairs):
            c_job, v_job, b_job = mix_a[3 * i:3 * i + 3]
            pair_c, done = narrow(c_job, "a")
            vc, _, sc = gather(pair_c, done)
            cp = act.run(lambda e, vc=vc: e.activation(cvpad[:, :, CONV_A - 1:], vc, ACT.Copy),
                         [sc, zero_pads, cv_free])
            slot_free[pair_c] = cp
            pair, done = narrow(v_job, "a")
            vv, _, s = gather(pair, done)
            cv = dve.run(lambda e, vv=vv: e.tensor_tensor(cvpad[:, :, CONV_A - 1:], cvpad[:, :, CONV_A - 1:], vv,
                                                          ALU.mult), [s, cp])
            slot_free[pair] = cv
            toks = [None, None]
            for k in range(CONV_A):
                for f in range(2):
                    j = 2 * i + f
                    if k == 0:
                        toks[f] = dve.run(lambda e, f=f, j=j: e.tensor_scalar(
                            conv3[:, f, :], cvpad[:, f, 0:TOKENS], column(ROW_CONV_A, j), None, ALU.mult),
                            [cv, cv_free])
                    else:
                        toks[f] = dve.run(lambda e, f=f, j=j, k=k: e.scalar_tensor_tensor(
                            conv3[:, f, :], cvpad[:, f, k:k + TOKENS], column(ROW_CONV_A + k, j), conv3[:, f, :],
                            ALU.mult, ALU.add), [toks[f]])
            pair, done = narrow(b_job, "a")
            vb, _, s = gather(pair, done)
            y = dve.run(lambda e, vb=vb: e.tensor_tensor(conv3, vb, conv3, ALU.mult), [s] + toks)
            slot_free[pair] = y
            cv_free = split_act("b", slice(2 * i, 2 * i + 2), BOTH, conv3, [y])


        def add_normed(half, got, row, buf, pause):
            n, h = wide_rows[:, half, :], resid[:, half, :]
            r = inverse_rms(half, D // WIDE, got)
            sq = []
            for c, cols in enumerate(PIECES):
                a = dve.run(lambda e, cols=cols: e.scalar_tensor_tensor(
                    h[:, cols], n[:, cols], rstd[:, half:half + 1], h[:, cols], ALU.mult, ALU.add), [r])
                sq.append(squares_of(half, c, h[:, cols], n[:, cols], [a]))
            r = inverse_rms(half, D // WIDE, sq)
            yield from turned(half, row, buf, r, sq, pause, 2)

        def take_normed(c, got, wide_free):
            def take(half, ps, done):
                a = dve.run(lambda e: e.tensor_tensor(wide_rows[:, half, PIECES[c]], ps, rows[0][:, PIECES[c]],
                                                      ALU.mult), [done, row_loaded[0]] + wide_free)
                row_used[0] = a
                b = squares_of(half, c, ps, partial[:, half, :], [a, part_free[half]])
                part_free[half] = b
                got[half] += [a, b]
                return a, b
            return take

        def mixed_and_rows():
            finish()
            load_row(0, t["mix_post_gain"][0], [cv_free] + mixed_done)
            load_row(1, t["mlp_pre_gain"][0], [cv_free] + mixed_done)

        got = [[], []]
        takes = [take_normed(c, got, mixed_done) for c in range(len(PIECES))]
        wide_in_two(early_proj[:EARLY], early_proj[EARLY:], "b", takes[:EARLY], mixed_and_rows)
        for job, take in zip(proj[:-1], takes[EARLY:]):
            wide(job, "b", take)
        wide_by_half(proj[-1:], "b", takes[-1:], 0, lambda: add_normed(0, got[0], 1, "a", 5))
        finish()

        def second_half_of_norm(got):
            def between():
                run_all(add_normed(1, got[1], 1, "a", 0))
            return between

        def take_up(s, c, pair, done):
            v, _, a = gather(pair, done)
            z = dve.run(lambda e: e.scalar_tensor_tensor(v, v, 0.0, v, ALU.max, ALU.mult), [a])
            k = (s % 2) * z_tiles + 2 * c
            slot_free[pair] = split_act("b", slice(k, k + 2), BOTH, v, [z])

        for dst, src in ((rope[:, :, :], t["c_rope"]), (masks[:, :, :], t["c_masks"]),
                         (counts[:, :, :], t["c_counts"])):
            consts = sp.run(lambda e, dst=dst, src=src: e.dma_start(dst, src), (), const_ready, 16)
        row_part = [[None] * (D // WIDE) for _ in range(HALVES)]
        got_mlp = [[], []]

        def take_down(s, c):
            def take(half, ps, done):
                dst = wide_rows[:, half, PIECES[c]]
                if s == 0:
                    a = act.run(lambda e: e.activation(dst, ps, ACT.Copy), [done] + turned_done)
                else:
                    a = dve.run(lambda e: e.tensor_tensor(dst, dst, ps, ALU.add), [done, row_part[half][c]])
                row_part[half][c] = a
                if s == supers - 1:
                    b = squares_of(half, c, dst, partial[:, half, :], [a, part_free[half]])
                    part_free[half] = b
                    d = dve.run(lambda e: e.tensor_tensor(dst, dst, rows[0][:, PIECES[c]], ALU.mult),
                                [b, row_loaded[0]])
                    row_used[0] = d
                    got_mlp[half].append(d)
                return (a,)
            return take

        narrow_by_half(up[0][0:2], "a", second_half_of_norm(got),
                       [lambda pair, done, c=c: take_up(0, c, pair, done) for c in range(2)])
        load_row(0, t["mlp_post_gain"][0], [])
        load_row(1, t["norm_a_2"][0], [])
        for c in range(2, len(up[0])):
            take_up(0, c, *narrow(up[0][c], "a"))
        for s in range(1, supers):
            for c, job in enumerate(up[s]):
                take_up(s, c, *narrow(job, "a"))
            for c, job in enumerate(down[s - 1]):
                wide(job, "b", take_down(s - 1, c), first=((s - 1) % 2) * z_tiles)
        s, first = supers - 1, ((supers - 1) % 2) * z_tiles
        for c in range(len(down[s]) - 2):
            wide(down[s][c], "b", take_down(s, c), first=first)
        wide_by_half(down[s][-2:], "b", [take_down(s, c) for c in range(len(down[s]) - 2, len(down[s]))], first,
                     lambda: add_normed(0, got_mlp[0], 1, "a", 5))
        finish()

        tiles_g = group_dim // P
        padded = TOKENS + POOL_PAD
        trio = [scratch[:, i * tiles_g * padded:(i + 1) * tiles_g * padded].rearrange("p (j n) -> p j n", j=tiles_g)
                for i in range(3)]
        u_buf, sum_a, sum_b = trio
        jobs_g = group_dim // NARROW

        def window_means(g, window, got_u):
            src, shift, toks, spare = u_buf, 1, got_u, [sum_a, sum_b]
            while shift < window:
                dst = spare[0]
                a = dve.run(lambda e, d=dst, s=src, k=shift: e.tensor_tensor(
                    d[:, :, POOL_PAD:], s[:, :, POOL_PAD:], s[:, :, POOL_PAD - k:POOL_PAD - k + TOKENS], ALU.add),
                    toks + [pool_free])
                spare = [spare[1], dst]
                src, toks, shift = dst, [a], 2 * shift
            other = spare[0]
            late, early = slice(2 * POOL_PAD, None), slice(POOL_PAD, 2 * POOL_PAD)
            a = dve.run(lambda e: e.scalar_tensor_tensor(other[:, :, late], src[:, :, late], 1.0 / window,
                                                         u_buf[:, :, late], ALU.mult, ALU.subtract), toks)
            divisors = counts[:, g, :].unsqueeze(1).to_broadcast([P, tiles_g, POOL_PAD])
            b = dve.run(lambda e: e.tensor_tensor(other[:, :, early], src[:, :, early], divisors, ALU.mult),
                        toks + [consts])
            b = dve.run(lambda e: e.tensor_tensor(other[:, :, early], other[:, :, early], u_buf[:, :, early],
                                                  ALU.subtract), [b])
            return split_act("b", slice(g * tiles_g, (g + 1) * tiles_g), BOTH, other[:, :, POOL_PAD:], [a, b])

        pool_free, got_u = None, []

        def take_u(i, pair, done):
            nonlocal pool_free
            if i == 0:
                for b in trio:
                    pool_free = dve.run(lambda e, b=b: e.memset(b[:, :, 0:POOL_PAD], 0.0), row_used)
            v, _, s = gather(pair, done)
            j = i % jobs_g
            a = act.run(lambda e: e.activation(u_buf[:, 2 * j:2 * j + 2, POOL_PAD:], v, ACT.Copy), [s, pool_free])
            slot_free[pair] = a
            got_u.append(a)
            if j == jobs_g - 1:
                pool_free = window_means(i // jobs_g, POOL_WINDOWS[i // jobs_g], got_u[-jobs_g:])

        narrow_by_half(pool_u[0:2], "a", second_half_of_norm(got_mlp),
                       [lambda pair, done, i=i: take_u(i, pair, done) for i in range(2)])
        for i in range(2, len(pool_u)):
            take_u(i, *narrow(pool_u[i], "a"))

        silu_gate = wide_rows[:, :, :].rearrange("p h (j n) -> p (h j) n", n=TOKENS)
        gate_done = [None] * KT

        def take_pool_gate(i, pair, done):
            v, _, s = gather(pair, done)
            dst = silu_gate[:, 2 * i:2 * i + 2, :]
            sg = act.run(lambda e: e.activation(dst, v, ACT.Tanh, scale=0.5), [s] + turned_done)
            a = dve.run(lambda e: e.scalar_tensor_tensor(dst, dst, 1.0, v, ALU.add, ALU.mult), [sg])
            slot_free[pair] = a
            for j in (2 * i, 2 * i + 1):
                gate_done[j] = act.run(lambda e, j=j: e.activation(
                    silu_gate[:, j, :], silu_gate[:, j, :], ACT.Copy,
                    scale=column(ROW_SCALE + j // TILES_A, j % TILES_A)), [a, features])

        for i, job in enumerate(pool_gate):
            take_pool_gate(i, *narrow(job, "a"))

        for g in range(n_pool):
            for i, job in enumerate(grp[g]):
                pair, done = narrow(job, "b", first=g * tiles_g)
                v, _, s = gather(pair, done)
                k = g * tiles_g + 2 * i
                a = dve.run(lambda e, k=k, v=v: e.tensor_tensor(v, v, silu_gate[:, k:k + 2, :], ALU.mult),
                            [s, gate_done[k], gate_done[k + 1]])
                slot_free[pair] = split_act("a", slice(k, k + 2), BOTH, v, [a])
        gated = slot_free[pair]

        load_row(0, t["norm_kv_2"], [pool_free])
        load_row(1, t["norm_b_2"][0], [pool_free])

        def take_added(c, got, after):
            def take(half, ps, done):
                h = resid[:, half, PIECES[c]]
                a = dve.run(lambda e: e.tensor_tensor(h, h, ps, ALU.add), [done] + after)
                got[half].append(squares_of(half, c, h, partial[:, half, :], [a, part_free[half]]))
                part_free[half] = got[half][-1]
                return (a,)
            return take

        got_a = [[], []]
        norm_a = [None, None]

        def norm_keys(half, pause):
            norm_a[half] = inverse_rms(half, D // WIDE, got_a[half])
            yield from turned(half, 0, "a", norm_a[half], [gated], pause)

        takes = [take_added(c, got_a, []) for c in range(len(proj_a))]
        for job, take in zip(proj_a[:-1], takes):
            wide(job, "a", take)
        wide_by_half(proj_a[-1:], "a", takes[-1:], 0, lambda: norm_keys(0, 2))
        finish()
        resid_dram = t["residual"].rearrange("(h p) n -> p h n", p=P)
        spill = [sp.run(lambda e, i=i: e.dma_start(resid_dram[:, i, :], resid[:, i, :]), got_a[i], spilled[i], 16)
                 for i in range(HALVES)]

        key_t = resid[:, :, :].rearrange("p h (j n) -> p (h j) n", n=TOKENS)
        query_t = scratch[:, 0:2 * GROUPS * 2 * TOKENS].rearrange("p (s g j n) -> p s g j n", s=2, g=GROUPS, j=2)
        mid = P // 2
        cos = rope[:, 0, :].unsqueeze(1).to_broadcast([P, 2, TOKENS])
        sin = rope[:, 1, :].unsqueeze(1).to_broadcast([P, 2, TOKENS])

        def take_rotated(dst, free, pair, done):
            return rotate(dst, free, pair, *gather(pair, done))

        def rotate(dst, free, pair, v, part, s):
            a = pool.run(lambda e: e.tensor_tensor(part, v, cos, ALU.mult), [s, consts])
            b = dve.run(lambda e: e.tensor_tensor(dst[0:mid], v[mid:P], sin[mid:P], ALU.mult), [s, consts] + free)
            c = dve.run(lambda e: e.tensor_tensor(dst[mid:P], v[0:mid], sin[0:mid], ALU.mult), [s, consts] + free)
            d = dve.run(lambda e: e.tensor_tensor(dst, dst, part, ALU.add), [a, b, c])
            slot_free[pair] = d
            part_free[pair] = d
            return d

        norm_b = {}

        def norm_queries(half):
            yield from turned(half, 1, "b", norm_a[half], [turned_done[half], gated], 1)

        def second_half_of_keys():
            run_all(norm_keys(1, 0))

        gathered = []

        def gather_key(pair, done):
            gathered.append((pair, *gather(pair, done)))

        narrow_by_half(keys[0:2], "a", second_half_of_keys, [gather_key, gather_key])
        key_done = []
        for half in range(HALVES):
            follow(norm_queries(half))
        for i, end in enumerate(gathered):
            key_done.append(rotate(key_t[:, 2 * i:2 * i + 2, :], spill + [row_used[1]], *end))
        for i in range(2, len(keys)):
            key_done.append(take_rotated(key_t[:, 2 * i:2 * i + 2, :], spill + [row_used[1]],
                                         *narrow(keys[i], "a")))

        val_done = []

        def take_value(c):
            def take(half, ps, done):
                val_done.append(act.run(lambda e: e.activation(wide_rows[:, half, PIECES[c]], ps, ACT.Copy),
                                        [done] + turned_done))
                return (val_done[-1],)
            return take
        for c, job in enumerate(vals):
            wide(job, "a", take_value(c))

        e0 = 2 * GROUPS * 2 * TOKENS
        e_buf = scratch[:, e0:e0 + 3 * GROUPS * P].rearrange("p (b n) -> p b n", b=3)
        pt_buf = turned_p_buf
        prev = {"e": None, "pt": gated}
        scored_last = [None, None]
        BLOCKS_OF = [slice(0, 1), slice(1, 3)]

        def attend(head, q, q_done):
            for _ in range(0 if head % 2 else 2):
                yield
            scored, weighed = [], []
            for half in range(HALVES):
                for blk in range(half + 1):
                    bank = half + blk
                    for g in range(GROUPS):
                        d = pe.run(lambda e, g=g, bank=bank, half=half, blk=blk: e.matmul(
                            aux[:, bank, g * P:(g + 1) * P], q[:, g, half * P:(half + 1) * P],
                            key_t[:, head, blk * P:(blk + 1) * P], start=True, stop=True),
                            q_done + key_done + [aux_free[bank]], silent=g < GROUPS - 1)
                scored.append(d)
            scored_last[(head // 2) % 2] = scored[1]
            softened = []
            for half, own in enumerate(BLOCKS_OF):
                ps = aux[:, own, 0:GROUPS * P]
                mask = masks[:, 1 - half:2, :]
                st = soft[:, half, :]
                a = dve.run(lambda e, ps=ps, mask=mask, own=own: e.scalar_tensor_tensor(
                    e_buf[:, own, :], ps, SCORE_SCALE, mask, ALU.mult, ALU.add), [scored[half], prev["e"], consts])
                for bank in range(own.start, own.stop):
                    aux_free[bank] = a
                m = dve.run(lambda e, own=own, st=st: e.tensor_reduce(st[:, 0:1], e_buf[:, own, :],
                                                                      mybir.AxisListType.XY, ALU.max), [a])
                m = dve.run(lambda e, st=st: e.tensor_scalar(st[:, 1:2], st[:, 0:1], -1.0, None, ALU.mult), [m])
                softened.append(act.run(lambda e, own=own, st=st: e.activation(
                    e_buf[:, own, :], e_buf[:, own, :], ACT.Exp, bias=st[:, 1:2], accum_out=st[:, 2:3]), [m]))
            e3 = e_buf.rearrange("p b (g n) -> p b g n", g=GROUPS)
            for half, own in enumerate(BLOCKS_OF):
                st = soft[:, half, :]
                r = dve.run(lambda e, st=st: e.reciprocal(st[:, 3:4], st[:, 2:3]), [softened[half]])
                w = e3[:, own, 0, :]
                for g in range(1, GROUPS):
                    r = dve.run(lambda e, w=w, own=own, g=g: e.tensor_tensor(w, w, e3[:, own, g, :], ALU.add), [r])
                weighed.append(act.run(lambda e, w=w, st=st: e.activation(w, w, ACT.Copy, scale=st[:, 3:4]), [r]))
            for _ in range(3):
                yield
            for blk in range(3):
                d = pe.run(lambda e, blk=blk: e.transpose(aux[:, 3, blk * P:(blk + 1) * P], e3[:, blk, 0, :],
                                                          ident[:, :]), weighed + [aux_free[3]], silent=blk < 2)
            prev["e"] = d
            c = act.run(lambda e: e.activation(pt_buf, aux[:, 3, 0:3 * P], ACT.Copy), [d, prev["pt"]])
            aux_free[3] = c
            for _ in range(1 if head < HEADS - 4 else 2):
                yield
            cols = slice(head * P, (head + 1) * P)
            pe.run(lambda e: e.matmul(aux[:, 0, 0:TOKENS], wide_rows[:, 0, cols], pt_buf[:, 0:2 * P],
                                      start=True, stop=False), [c, aux_free[0]] + val_done, silent=True)
            d = pe.run(lambda e: e.matmul(aux[:, 0, P:2 * P], wide_rows[:, 1, cols], pt_buf[:, 2 * P:3 * P],
                                          start=False, stop=True))
            prev["pt"] = d
            aux_free[0] = split_act("a", slice(head, head + 1), BOTH, aux[:, 0:1, 0:TOKENS], [d])
            yield

        for b in range(batches):
            q_done = []
            for g, job in enumerate(queries[b]):
                end = narrow(job, "b")
                if g == 0 and b >= 2:
                    while attended[0] < 2 * (b - 1):
                        step()
                q_done.append(take_rotated(query_t[:, b % 2, g, :, :], [scored_last[b % 2], row_used[1], row_used[0]],
                                           *end))
            if b == 0:
                attended = [0]

            def counted(steps):
                yield from steps
                attended[0] += 1
            for j in range(2):
                beside.append(counted(attend(2 * b + j, query_t[:, b % 2, :, j, :], q_done)))

        for i, job in enumerate(gates):
            pair, done = narrow(job, "b")
            while attended[0] < 2 * (i + 1):
                step()
            v, part, s = gather(pair, done)
            k = slice(2 * i, 2 * i + 2)
            sg = act.run(lambda e, v=v, part=part: e.activation(part, v, ACT.Tanh, scale=0.5), [s])
            a = dve.run(lambda e, v=v, part=part: e.scalar_tensor_tensor(v, part, 1.0, v, ALU.add, ALU.mult), [sg])
            whole = dve.run(lambda e, k=k, part=part: e.tensor_tensor(part, act_a[:, k, 0, :].bitcast(F32),
                                                                      act_a[:, k, 1, :].bitcast(F32), ALU.add),
                            [a] + [x for kt in (2 * i, 2 * i + 1) for x in ready["a"][kt][0]])
            y = dve.run(lambda e, v=v, part=part: e.tensor_tensor(v, v, part, ALU.mult), [whole])
            part_free[pair] = y
            slot_free[pair] = split_act("a", k, BOTH, v, [y], 0.5)
            if i == len(gates) - 2:
                finish()
                load_row(0, t["norm_f_2"], scored_last)
                reload_ = sp.run(lambda e: e.dma_start(resid[:, :, :], resid_dram), spill + scored_last, reloaded, 16)

        out_v = out.rearrange("b (h p) n -> p (b h) n", p=P)
        got_b = [[], []]

        def final_norm(half):
            h, n = resid[:, half, :], wide_rows[:, half, :]
            r = inverse_rms(half, D // WIDE, got_b[half])
            for cols in PIECES:
                s = dve.run(lambda e, cols=cols: e.scalar_tensor_tensor(
                    n[:, cols], h[:, cols], rstd[:, half:half + 1], rows[0][:, cols], ALU.mult, ALU.mult),
                    [r, row_loaded[0], prev["pt"]])
                sp.run(lambda e, cols=cols: e.dma_start(out_v[:, half, cols], n[:, cols]), [s], stored, 16)
            yield

        takes = [take_added(c, got_b, [reload_]) for c in range(len(proj_b))]
        for job, take in zip(proj_b[:-1], takes):
            wide(job, "a", take)
        wide_by_half(proj_b[-1:], "a", takes[-1:], 0, lambda: final_norm(0))
        run_all(final_norm(1))
        for s in (stored, spilled[0], spilled[1]):
            sp.run(None, [(s, s.count)], silent=True)

        block = ctx.enter_context(nc.Block())

        @block.sync
        def _(e):
            sp.emit(e)

        @block.scalar
        def _(e):
            act.emit(e)

        @block.vector
        def _(e):
            dve.emit(e)

        @block.gpsimd
        def _(e):
            pool.emit(e)

        @block.tensor
        def _(e):
            pe.emit(e)


_INS = ["x", "mix_pre_gain", "w_in", "conv_a_w", "conv_b_w", "conv_b_bias", "ln_b_gain", "ln_b_bias", "w_out",
        "mix_post_gain", "mlp_pre_gain", "w_up", "w_down", "mlp_post_gain", "norm_a_2", "w_in_a_2", "w_grp_a_2",
        "scale_a_2", "w_out_a_2", "norm_kv_2", "w_k_2", "w_v_2", "norm_b_2", "w_in_b_2", "w_out_b_2", "norm_f_2"]


def shape_constants():
    f = np.float32
    inv_freq = (f(1.0) / (f(10000.0) ** (np.arange(0, P, 2, dtype=f) / f(P)))).astype(f)
    ang = np.arange(TOKENS, dtype=f)[:, None] * inv_freq[None, :]
    cos, sin = np.cos(ang).astype(f), np.sin(ang).astype(f)
    rope = np.stack([np.concatenate([cos.T, cos.T]), np.concatenate([sin.T, -sin.T])], axis=1)
    q = np.arange(P)[:, None]
    k = np.arange(P)[None, :]
    masks = np.zeros((P, 2, GROUPS, P), f)
    for b, shift in enumerate((P, 0)):
        back = q + shift - k
        for g, d in enumerate(DILATIONS):
            seen = (back >= 0) & (back % d == 0) & (back <= REACH * d)
            masks[:, b, g, :] = np.where(seen, 0.0, MASKED)
    counts = np.zeros((P, len(POOL_WINDOWS), POOL_PAD), f)
    for g, w in enumerate(POOL_WINDOWS):
        counts[:, g, :] = f(1.0) / np.minimum(np.arange(1, POOL_PAD + 1), w).astype(f)
    return {"c_ident": np.eye(P, dtype=f), "c_rope": np.ascontiguousarray(rope),
            "c_masks": masks.reshape(P, 2, GROUPS * P).astype(mybir.dt.np(mybir.dt.bfloat16)), "c_counts": counts}


def kernel(**inputs):
    import concourse.bacc as bacc
    from concourse.bass_utils import run_bass_kernel_spmd

    nc = bacc.Bacc("TRN2", target_bir_lowering=False, num_devices=1)
    arrays, tensors = {}, {}
    given = {name: np.ascontiguousarray(inputs[name]) for name in _INS}
    given.update(shape_constants())
    for name, a in given.items():
        arrays[f"in_{name}"] = a
        tensors[name] = nc.dram_tensor(f"in_{name}", a.shape, mybir.dt.from_np(a.dtype), kind="ExternalInput").ap()
    tensors["residual"] = nc.dram_tensor("residual", (TOKENS, D), F32).ap()
    out = nc.dram_tensor("out_0", (1, TOKENS, D), F32, kind="ExternalOutput").ap()
    build(nc, tensors, out)
    got = run_bass_kernel_spmd(nc, [arrays], core_ids=[0])
    return got.results[0]["out_0"]
```
